# Optimizing a Trainium2 kernel written in Bass

```python
import math
import jax, jax.numpy as jnp
from jax import lax
import numpy as np

D_MODEL = 1024
BATCH = 1
SEQ = 512
DEPTH = 2

CHUNK = 64
Q_BLOCK = 128
EPS = 1e-5
D_FF = ((8 * D_MODEL // 3 + 127) // 128) * 128
N_A_LAYERS = DEPTH // 2
N_B_LAYERS = DEPTH - N_A_LAYERS
SSM_EXPAND = 2
SSM_D_INNER = SSM_EXPAND * D_MODEL
SSM_HEAD_DIM = 64
SSM_HEADS = SSM_D_INNER // SSM_HEAD_DIM
SSM_GROUPS = 8
SSM_HEADS_PER_GROUP = SSM_HEADS // SSM_GROUPS
SSM_STATE = 128
SSM_CONV = 4
SSM_BLOCK = CHUNK
SSM_CONV_DIM = SSM_D_INNER + 2 * SSM_GROUPS * SSM_STATE
SSM_IN_DIM = SSM_D_INNER + SSM_CONV_DIM + SSM_HEADS
DIFF_HEAD_DIM = 64
DIFF_HEADS = D_MODEL // (2 * DIFF_HEAD_DIM)
DIFF_QK_DIM = DIFF_HEADS * 2 * DIFF_HEAD_DIM
DIFF_V_DIM = DIFF_HEADS * 2 * DIFF_HEAD_DIM
ROPE_THETA = 10000.0

kernel_name = "yoco_mamba2_diffattn_macaron"

def rms_norm(x, g):
    xf = x.astype(jnp.float32)
    y = xf * lax.rsqrt(jnp.mean(xf * xf, axis=-1, keepdims=True) + EPS)
    return (y * g.astype(jnp.float32)).astype(x.dtype)

def swiglu_ffn(h, w_in, w_out):
    gate, up = jnp.split(h @ w_in, 2, axis=-1)
    return (jax.nn.silu(gate) * up) @ w_out

def rope_tables(seq_len, dim):
    inv = ROPE_THETA ** (-jnp.arange(0, dim, 2, dtype=jnp.float32) / dim)
    ang = jnp.arange(seq_len, dtype=jnp.float32)[:, None] * inv[None, :]
    return jnp.cos(ang), jnp.sin(ang)

def apply_rope(x, cos, sin):
    xf = x.astype(jnp.float32)
    x1, x2 = jnp.split(xf, 2, axis=-1)
    c = cos[None, :, None, None, :]
    s = sin[None, :, None, None, :]
    return jnp.concatenate([x1 * c - x2 * s, x2 * c + x1 * s], axis=-1).astype(x.dtype)

def causal_depthwise_conv(x, w, b):
    y = lax.conv_general_dilated(
        x, w[:, None, :].astype(x.dtype), window_strides=(1,),
        padding=[(SSM_CONV - 1, 0)], dimension_numbers=('NWC', 'WIO', 'NWC'),
        feature_group_count=x.shape[-1])
    return y + b.astype(x.dtype)

def ssd_scan(x, dt, a, b_in, c_in):
    bsz, s = x.shape[0], x.shape[1]
    nc = s // SSM_BLOCK
    L, G, Hg, P, N = SSM_BLOCK, SSM_GROUPS, SSM_HEADS_PER_GROUP, SSM_HEAD_DIM, SSM_STATE
    x = x.reshape(bsz, nc, L, G, Hg, P)
    dt = dt.reshape(bsz, nc, L, G, Hg)
    b = b_in.reshape(bsz, nc, L, G, N)
    c = c_in.reshape(bsz, nc, L, G, N)
    a_cum = jnp.cumsum(dt * a, axis=2)
    xdt = x * dt[..., None]
    seg = a_cum[:, :, :, None] - a_cum[:, :, None, :]
    causal = jnp.tril(jnp.ones((L, L), dtype=bool))[None, None, :, :, None, None]
    decay = jnp.exp(jnp.where(causal, seg, -jnp.inf))
    cb = jnp.einsum('bclgn,bcsgn->bclsg', c, b)
    y_diag = jnp.einsum('bclsg,bclsgh,bcsghp->bclghp', cb, decay, xdt)
    decay_to_end = jnp.exp(a_cum[:, :, -1:] - a_cum)
    states = jnp.einsum('bclgn,bclgh,bclghp->bcghpn', b, decay_to_end, xdt)
    chunk_decay = jnp.exp(a_cum[:, :, -1])

    def step(h, inp):
        st, dec = inp
        return h * dec[..., None, None] + st, h

    h0 = jnp.zeros((bsz, G, Hg, P, N), jnp.float32)
    _, prev = lax.scan(step, h0, (jnp.moveaxis(states, 1, 0), jnp.moveaxis(chunk_decay, 1, 0)))
    y_off = jnp.einsum('bclgn,cbghpn,bclgh->bclghp', c, prev, jnp.exp(a_cum))
    return (y_diag + y_off).reshape(bsz, s, G, Hg, P)

def mamba2_mixer(h, w_in, conv_w, conv_b, dt_bias, a_log, d_skip, norm_g, w_out):
    bsz, s, _ = h.shape
    G, Hg, P, N = SSM_GROUPS, SSM_HEADS_PER_GROUP, SSM_HEAD_DIM, SSM_STATE
    proj = h @ w_in
    z, xbc, dt = jnp.split(proj, [SSM_D_INNER, SSM_D_INNER + SSM_CONV_DIM], axis=-1)
    xbc = jax.nn.silu(causal_depthwise_conv(xbc, conv_w, conv_b))
    xs, b_in, c_in = jnp.split(xbc, [SSM_D_INNER, SSM_D_INNER + G * N], axis=-1)
    xs = xs.astype(jnp.float32).reshape(bsz, s, G, Hg, P)
    b_in = b_in.astype(jnp.float32).reshape(bsz, s, G, N)
    c_in = c_in.astype(jnp.float32).reshape(bsz, s, G, N)
    dt = jax.nn.softplus(dt.astype(jnp.float32) + dt_bias.astype(jnp.float32)).reshape(bsz, s, G, Hg)
    a = -jnp.exp(a_log.astype(jnp.float32)).reshape(G, Hg)
    y = ssd_scan(xs, dt, a, b_in, c_in) + d_skip.astype(jnp.float32).reshape(G, Hg)[:, :, None] * xs
    yg = (y.reshape(bsz, s, SSM_D_INNER) * jax.nn.silu(z.astype(jnp.float32))).reshape(bsz, s, G, SSM_D_INNER // G)
    yg = yg * lax.rsqrt(jnp.mean(yg * yg, axis=-1, keepdims=True) + EPS)
    y = (yg.reshape(bsz, s, SSM_D_INNER) * norm_g.astype(jnp.float32)).astype(h.dtype)
    return y @ w_out

def shared_kv(x, kv_norm, w_kv, cos, sin):
    bsz, s, _ = x.shape
    kv = rms_norm(x, kv_norm) @ w_kv
    k, v = jnp.split(kv, [DIFF_QK_DIM], axis=-1)
    k = apply_rope(k.reshape(bsz, s, DIFF_HEADS, 2, DIFF_HEAD_DIM), cos, sin)
    v = v.reshape(bsz, s, DIFF_HEADS, 2 * DIFF_HEAD_DIM)
    return k, v

def diff_attention(h, k, v, w_q, lam, subln_g, w_o, lambda_init, cos, sin):
    bsz, s, _ = h.shape
    q = apply_rope((h @ w_q).reshape(bsz, s, DIFF_HEADS, 2, DIFF_HEAD_DIM), cos, sin)
    lamf = lam.astype(jnp.float32)
    lam_full = (jnp.exp(jnp.sum(lamf[0] * lamf[1])) - jnp.exp(jnp.sum(lamf[2] * lamf[3]))
                + lambda_init)
    nb = s // Q_BLOCK
    q_blocks = jnp.moveaxis(q.reshape(bsz, nb, Q_BLOCK, DIFF_HEADS, 2, DIFF_HEAD_DIM), 1, 0)
    key_chunk = jnp.arange(s) // CHUNK
    scale = DIFF_HEAD_DIM ** -0.5

    def block(args):
        qb, i = args
        q_chunk = (i * Q_BLOCK + jnp.arange(Q_BLOCK)) // CHUNK
        mask = key_chunk[None, :] <= q_chunk[:, None]
        logits = jnp.einsum('bqhmd,bkhmd->bhmqk', qb, k).astype(jnp.float32) * scale
        p = jax.nn.softmax(jnp.where(mask, logits, -jnp.inf), axis=-1)
        w = p[:, :, 0] - lam_full * p[:, :, 1]
        return jnp.einsum('bhqk,bkhe->bqhe', w.astype(v.dtype), v)

    o = lax.map(block, (q_blocks, jnp.arange(nb)))
    o = jnp.moveaxis(o, 0, 1).reshape(bsz, s, DIFF_HEADS, 2 * DIFF_HEAD_DIM)
    o = rms_norm(o, subln_g) * (1.0 - lambda_init)
    return o.reshape(bsz, s, DIFF_V_DIM) @ w_o

def setup_inputs(seed: int = 0) -> dict:
    key = jax.random.key(seed)
    ks = iter(jax.random.split(key, 32))
    f32 = jnp.float32

    def nrm(shape, fan_in):
        return jax.random.normal(next(ks), shape, f32) * (fan_in ** -0.5)

    def gain(shape):
        return 1.0 + 0.02 * jax.random.normal(next(ks), shape, f32)

    x = jax.random.normal(next(ks), (BATCH, SEQ, D_MODEL), f32)
    dt0 = jnp.exp(jax.random.uniform(next(ks), (N_A_LAYERS, SSM_HEADS), f32,
                                     math.log(1e-3), math.log(1e-1)))
    return {
        "x": x,
        "ffn1_norm": gain((DEPTH, D_MODEL)),
        "ffn1_w_in": nrm((DEPTH, D_MODEL, 2 * D_FF), D_MODEL),
        "ffn1_w_out": nrm((DEPTH, D_FF, D_MODEL), D_FF),
        "mixer_norm": gain((DEPTH, D_MODEL)),
        "ffn2_norm": gain((DEPTH, D_MODEL)),
        "ffn2_w_in": nrm((DEPTH, D_MODEL, 2 * D_FF), D_MODEL),
        "ffn2_w_out": nrm((DEPTH, D_FF, D_MODEL), D_FF),
        "ssm_w_in": nrm((N_A_LAYERS, D_MODEL, SSM_IN_DIM), D_MODEL),
        "ssm_conv_w": nrm((N_A_LAYERS, SSM_CONV, SSM_CONV_DIM), SSM_CONV),
        "ssm_conv_b": 0.02 * jax.random.normal(next(ks), (N_A_LAYERS, SSM_CONV_DIM), f32),
        "ssm_dt_bias": dt0 + jnp.log(-jnp.expm1(-dt0)),
        "ssm_a_log": jnp.log(jax.random.uniform(next(ks), (N_A_LAYERS, SSM_HEADS), f32, 1.0, 16.0)),
        "ssm_d": 1.0 + 0.1 * jax.random.normal(next(ks), (N_A_LAYERS, SSM_HEADS), f32),
        "ssm_norm": gain((N_A_LAYERS, SSM_D_INNER)),
        "ssm_w_out": nrm((N_A_LAYERS, SSM_D_INNER, D_MODEL), SSM_D_INNER),
        "kv_norm": gain((D_MODEL,)),
        "w_kv": nrm((D_MODEL, DIFF_QK_DIM + DIFF_V_DIM), D_MODEL),
        "attn_w_q": nrm((N_B_LAYERS, D_MODEL, DIFF_QK_DIM), D_MODEL),
        "attn_lambda": 0.1 * jax.random.normal(next(ks), (N_B_LAYERS, 4, DIFF_HEAD_DIM), f32),
        "attn_subln": gain((N_B_LAYERS, 2 * DIFF_HEAD_DIM)),
        "attn_w_o": nrm((N_B_LAYERS, DIFF_V_DIM, D_MODEL), DIFF_V_DIM),
        "final_norm": gain((D_MODEL,)),
    }

def reference(x, ffn1_norm, ffn1_w_in, ffn1_w_out, mixer_norm, ffn2_norm, ffn2_w_in,
              ffn2_w_out, ssm_w_in, ssm_conv_w, ssm_conv_b, ssm_dt_bias, ssm_a_log, ssm_d,
              ssm_norm, ssm_w_out, kv_norm, w_kv, attn_w_q, attn_lambda, attn_subln,
              attn_w_o, final_norm):
    s = x.shape[1]
    cos, sin = rope_tables(s, DIFF_HEAD_DIM)
    shared_k, shared_v = None, None
    for layer in range(DEPTH):
        x = x + 0.5 * swiglu_ffn(rms_norm(x, ffn1_norm[layer]), ffn1_w_in[layer], ffn1_w_out[layer])
        hm = rms_norm(x, mixer_norm[layer])
        if layer < N_A_LAYERS:
            i = layer
            x = x + mamba2_mixer(hm, ssm_w_in[i], ssm_conv_w[i], ssm_conv_b[i], ssm_dt_bias[i],
                                 ssm_a_log[i], ssm_d[i], ssm_norm[i], ssm_w_out[i])
        else:
            j = layer - N_A_LAYERS
            lambda_init = 0.8 - 0.6 * math.exp(-0.3 * layer)
            x = x + diff_attention(hm, shared_k, shared_v, attn_w_q[j], attn_lambda[j],
                                   attn_subln[j], attn_w_o[j], lambda_init, cos, sin)
        x = x + 0.5 * swiglu_ffn(rms_norm(x, ffn2_norm[layer]), ffn2_w_in[layer], ffn2_w_out[layer])
        if layer == N_A_LAYERS - 1:
            shared_k, shared_v = shared_kv(x, kv_norm, w_kv, cos, sin)
    return rms_norm(x, final_norm)


_drawn_inputs = setup_inputs


def setup_inputs(seed=0):
    import zlib

    import numpy as np

    out = dict(_drawn_inputs(seed))
    spreads = {}
    factors = {'ffn1_norm': 4.29,
     'ffn2_norm': 6.773,
     'ssm_norm': 3.407,
     'kv_norm': 18.367,
     'attn_subln': 59.008,
     'final_norm': 7.994}
    for name, (base, spread) in spreads.items():
        noise = np.random.default_rng([zlib.crc32(name.encode()), seed]).standard_normal(out[name].shape)
        drawn = base * np.exp(spread * noise) if base else spread * noise
        out[name] = __import__('jax').numpy.asarray(drawn.astype(out[name].dtype))
    for name, factor in factors.items():
        out[name] = (out[name] * factor).astype(out[name].dtype)
    return out
```

```python
from contextlib import ExitStack
import math

import numpy as np
import concourse.bass as bass
from concourse import mybir

F32 = mybir.dt.float32
F32R = mybir.dt.float32r
ALU = mybir.AluOpType
ACT = mybir.ActivationFunctionType
AXX = mybir.AxisListType.X

P = 128
S = 512
D = 1024
KD = D // P
F = 2816
KF = F // P
DI = 2048
GROUPS = 8
HG = 4
HEADS = 32
HP = 64
NST = 128
KI = DI // P
L = 128
NC = S // L
EPS = 1e-5
AH = 8
CHUNK = 64
LAMBDA_INIT = 0.8 - 0.6 * math.exp(-0.3)
SCALE = 64 ** -0.5

SLOTS = 4
UK = 4
LEAD = 3

PHASES = [("in0", 22, 2), ("out0", 4, 6), ("ssm", 24, 2), ("sout", 4, 4), ("in1", 22, 2),
          ("out1", 4, 6), ("kv", 8, 2), ("in2", 22, 2), ("out2", 4, 6), ("q", 4, 2), ("wo", 4, 2),
          ("in3", 22, 2), ("out3", 4, 6)]
X_PAIRS = KD // 2


def plan(stop):
    unit, pair, at = 0, X_PAIRS, {}
    phases = []
    for name, pairs, units in PHASES:
        assert unit % SLOTS == 0 and pair % 2 == 0
        at[name] = (unit, pair, pairs, units)
        phases.append(name)
        unit += pairs * units
        pair += pairs
        if name == stop:
            break
    return at, phases, unit


def build_trunk(nc, t, stop=None):
    at, phases, n_units = plan(stop)
    last = phases[-1]
    ctx = ExitStack()
    with ctx:
        base = (nc.sbuf_base + 63) // 32 * 32
        end = nc.sbuf_top

        class Region:

            def __init__(self, start, size):
                self.at, self.end = start, start + size

            def tile(self, name, shape, dtype=F32):
                size = 4 * math.prod(shape[1:])
                size = (size + 31) // 32 * 32
                assert self.at + size <= self.end, (name, self.at + size - self.end)
                got = nc.alloc_sbuf_tensor_at(name, shape, dtype, offset=self.at)
                self.at += size
                return got

        glob = Region(base, end - base)
        arena_size = 2 * KF * S * 4
        x = glob.tile("x_t", [P, KD, S])
        xh_off = glob.at
        xh = glob.tile("x_hi", [P, KD, S], F32R)
        xl = glob.tile("x_lo", [P, KD, S], F32R)
        raw = [glob.tile(f"w_raw{s}", [P, UK * 256]) for s in range(SLOTS)]
        whi = [glob.tile(f"w_hi{s}", [P, UK * 256], F32R) for s in range(SLOTS)]
        wlo = [glob.tile(f"w_lo{s}", [P, UK * 256], F32R) for s in range(SLOTS)]
        rstd = glob.tile("rstd", [P, S])
        rms_tok = glob.tile("rms_tok", [P, S // P])
        inv_tok = glob.tile("inv_rms_tok", [P, S // P])
        buf_a = glob.tile("gate_or_squares", [P, 2, S])
        buf_b = glob.tile("up_or_square_sum", [P, 2, S])
        ident = glob.tile("ident", [P, P])
        ones = glob.tile("ones", [P, P])
        NG = 16 + 16 + 16 + 8 + 8 + 16 + 32 + 1
        gains = glob.tile("gains", [P, NG])
        arena_off = glob.at
        assert arena_off + arena_size <= end, (arena_off, arena_size, end)
        rest = Region(arena_off + arena_size, end - arena_off - arena_size)

        ffn = Region(arena_off, arena_size)
        hh = ffn.tile("hidden_hi", [P, KF, S], F32R)
        hl = ffn.tile("hidden_lo", [P, KF, S], F32R)
        first = Region(arena_off, arena_size)
        x_in = first.tile("x_in", [P, S // P, D])
        gain_rows = first.tile("gain_rows", [NG, P])
        x_out = first.tile("x_out", [P, S // P, D])

        conv_rows = first.tile("conv_rows", [P, P])

        ssm = Region(arena_off, arena_size)
        y32 = ssm.tile("y_t", [P, KI, S])
        group_off = ssm.at
        PRE = S + 4
        pre = ssm.tile("conv_in", [P, 4, PRE])
        dt_off = ssm.at
        xbc = ssm.tile("conv_out", [P, 4, S])
        segm = ssm.tile("decay_or_m", [P, HG, S])
        cumb = ssm.tile("cum_or_c", [P, HG, S])
        tanh = ssm.tile("tanh", [P, 4, S])
        xdt = ssm.tile("x_dt", [P, NC, HG * HP])
        xde = ssm.tile("x_dt_to_end", [P, NC, HG * HP])
        btok = ssm.tile("b_tok", [P, NC, NST])
        ysq = ssm.tile("y_squares", [P, 2, S])
        ssm_tanh_z = tanh[:, 0:2, :]
        cbm = rest.tile("cb_masked", [P, S])
        prev = rest.tile("state_before", [P, NC - 1, HG * HP])
        cw = rest.tile("conv_w_b", [P, 5, 32])
        dskip = rest.tile("d_skip", [P, KI])
        mask = rest.tile("causal", [P, P])
        tok_all = rest.tile("cum_dt_tok", [P, 2, NC, HEADS])
        gtok = rest.tile("cum_dt_group", [P, 2, NC, HG])
        dte = rest.tile("to_end", [P, NC, HG])
        cd = rest.tile("block_decay", [P, HG, NC])
        gcw = [rest.tile(f"group_conv{r}", [P, 5, 4]) for r in range(2)]
        gdn = [rest.tile(f"group_d_norm{r}", [P, 2, 2]) for r in range(2)]
        dt_bias = rest.tile("dt_bias", [P, 1])
        a_neg = rest.tile("minus_a", [P, 1])
        yrms = rest.tile("y_rms", [P, NC])
        yinv = rest.tile("y_inv_rms", [P, NC])
        DT0 = P - HEADS
        dtr = Region(dt_off, arena_off + arena_size - dt_off)
        wdt = dtr.tile("w_dt", [P, KD, P])
        wdt_hi = dtr.tile("w_dt_hi", [P, KD, P], F32R)
        wdt_lo = dtr.tile("w_dt_lo", [P, KD, P], F32R)
        dt_raw = dtr.tile("dt_raw", [P, S])
        dt_e = dtr.tile("dt_e", [P, S])
        dt_u = dtr.tile("dt_u", [P, S])
        dt_ln = dtr.tile("dt_ln", [P, S])
        dt_r = dtr.tile("dt_r", [P, S])
        dt_t = dtr.tile("dt_t", [P, S])
        dt_c = dtr.tile("dt_c", [P, S])
        y_hi = Region(group_off, KI * S * 4).tile("y_hi", [P, KI, S], F32R)
        y_lo = Region(arena_off, KI * S * 4).tile("y_lo", [P, KI, S], F32R)
        rope = Region(arena_off, arena_size)
        cos_t = rope.tile("cos_t", [P, S])
        sin_t = rope.tile("sin_t", [P, S])
        rot = rope.tile("rot", [P, P])
        heads_out = [rope.tile(f"heads_out{r}", [P, 2, S]) for r in range(2)]
        att = Region(arena_off, arena_size)
        o_all = att.tile("o_t", [P, AH, S])
        o_hi = att.tile("o_hi", [P, AH, S], F32R)
        o_lo = att.tile("o_lo", [P, AH, S], F32R)
        q_cur = [att.tile(f"q_cur{r}", [P, S]) for r in range(2)]
        k_cur = [att.tile(f"k_cur{r}", [P, S]) for r in range(2)]
        v_cur = [att.tile(f"v_cur{r}", [P, NC, P]) for r in range(2)]
        probs = [att.tile(f"probs{r}", [P, 2, S]) for r in range(2)]
        w_t = [att.tile(f"w_t{r}", [P, S]) for r in range(2)]
        osq = att.tile("o_squares", [P, S])
        lam_in = att.tile("lam_in", [P, 4, HP])
        lam_pr = att.tile("lam_products", [P, 2, HP])
        lam_s = rest.tile("lam_sums", [P, 2])
        lam = rest.tile("lam", [P, 1])
        mx = [rest.tile(f"row_max{r}", [P, 2]) for r in range(2)]
        nb = [rest.tile(f"minus_max{r}", [P, 2]) for r in range(2)]
        rs = [rest.tile(f"row_sum{r}", [P, 2]) for r in range(2)]
        ri = [rest.tile(f"row_inv{r}", [P, 2]) for r in range(2)]
        c1 = [rest.tile(f"lam_inv{r}", [P, 1]) for r in range(2)]
        orms = rest.tile("o_rms", [P, AH, NC])
        oinv = rest.tile("o_inv_rms", [P, AH, NC])
        g_sub = rest.tile("subln_gain", [P, 1])
        q_dram = nc.dram_tensor("q_scratch", [AH, P, S], F32, kind="Internal").ap()
        k_dram = nc.dram_tensor("k_scratch", [AH, P, S], F32, kind="Internal").ap()
        v_dram = nc.dram_tensor("v_scratch", [AH, P, S], F32, kind="Internal").ap()
        cum_dram = nc.dram_tensor("cum_scratch", [HEADS, S], F32, kind="Internal").ap()

        G = {}
        col = 0
        for name, n in (("ffn1", 16), ("mixer", 16), ("ffn2", 16), ("kv", 8), ("final", 8),
                        ("ssm_norm", 16), ("conv_b", 32), ("subln", 1)):
            G[name] = col
            col += n

        pw = ctx.enter_context(nc.psum_tensor("psum_pairs", [P, 4, S], F32))
        pa = ctx.enter_context(nc.psum_tensor("psum_other", [P, 4, S], F32))

        def sem(name):
            return ctx.enter_context(nc.semaphore(name))

        unit_loaded = [sem(f"unit_loaded{s}") for s in range(SLOTS)]
        hi_ready = sem("hi_ready")
        lo_ready = sem("lo_ready")
        unit_used = sem("unit_used")
        pair_free = sem("pair_free")
        consts_loaded = sem("consts_loaded")
        x_loaded = sem("x_loaded")
        const_made = sem("const_made")
        gains_turned = sem("gains_turned")
        gains_ready = sem("gains_ready")
        x_turned = sem("x_turned")
        x_hi_ready = sem("x_hi_ready")
        x_split = sem("x_split")
        squared = sem("squared")
        sum_cleared = sem("sum_cleared")
        summed = sem("summed")
        stat_ready = sem("stat_ready")
        rms_ready = sem("rms_ready")
        inv_ready = sem("inv_ready")
        spread_ready = sem("spread_ready")
        rstd_ready = sem("rstd_ready")
        silu_done = sem("silu_done")
        up_scaled = sem("up_scaled")
        hid_made = sem("hid_made")
        hid_hi = sem("hid_hi")
        hid_ready = sem("hid_ready")
        y_normed = sem("y_normed")
        y_turned = sem("y_turned")
        y_copied = sem("y_copied")
        stored = sem("stored")
        rope_loaded = sem("rope_loaded")
        head_rotated = sem("head_rotated")
        rope_cos = sem("rope_cos")
        rope_sin = sem("rope_sin")
        heads_ready = sem("heads_ready")
        heads_stored = [sem(f"heads_stored{r}") for r in range(2)]
        lam_loaded = sem("lam_loaded")
        lam_step = sem("lam_step")
        lam_exp = sem("lam_exp")
        head_loaded = [sem(f"head_loaded{r}") for r in range(2)]
        logits_ready = sem("logits_ready")
        masked = sem("masked")
        max_ready = sem("max_ready")
        bias_ready = sem("bias_ready")
        exp_ready = sem("exp_ready")
        inv_rows = sem("inv_rows")
        lam_rows = sem("lam_rows")
        second_ready = sem("second_ready")
        w_ready = sem("w_ready")
        w_turned = sem("w_turned")
        wt_ready = sem("wt_ready")
        pv_done = sem("pv_done")
        o_copied = sem("o_copied")
        o_squared = sem("o_squared")
        o_summed = sem("o_summed")
        o_rms_ready = sem("o_rms_ready")
        o_inv_ready = sem("o_inv_ready")
        o_spread = sem("o_spread")
        o_normed = sem("o_normed")
        o_hi_ready = sem("o_hi_ready")
        o_split = sem("o_split")
        ssm_consts = sem("ssm_consts")
        conv_turned = sem("conv_turned")
        cw_ready = sem("cw_ready")
        wdt_loaded = sem("wdt_loaded")
        wdt_hi_ready = sem("wdt_hi_ready")
        wdt_ready = sem("wdt_ready")
        dt_used = sem("dt_product")
        dt_v = sem("dt_vector_step")
        dt_s = sem("dt_scalar_step")
        cum_stored = sem("cum_stored")
        cum_ready = sem("cum_ready")
        tok_turned = sem("tok_turned")
        tok_ready = sem("tok_ready")
        halo_ready = sem("halo_ready")
        params_ready = sem("params_ready")
        cum_loaded = sem("cum_loaded")
        conv_base = sem("conv_base")
        conv_tap = sem("conv_tap")
        conv_tanh = sem("conv_tanh")
        conv_done = sem("conv_done")
        z_tanh = sem("z_tanh")
        z_ready = sem("z_ready")
        gtok_ready = sem("gtok_ready")
        dte_diff = sem("dte_diff")
        dte_ready = sem("dte_ready")
        seg_ready = sem("seg_ready")
        decay_ready = sem("decay_ready")
        growth_ready = sem("growth_ready")
        cd_ready = sem("cd_ready")
        turned_a = sem("x_b_turned")
        cb_product = sem("cb_product")
        btok_ready = sem("btok_ready")
        xdt_ready = sem("xdt_ready")
        cbm_ready = sem("cbm_ready")
        xde_ready = sem("xde_ready")
        m_ready = sem("m_ready")
        c_ready = sem("c_ready")
        states_product = sem("states_product")
        prev_step = sem("prev_step")
        y_product = sem("y_product")
        y_plus = sem("y_plus_skip")
        y_gated = sem("y_gated")
        y_squared = sem("y_squared")
        y_stat = sem("y_stat")
        y_rms = sem("y_rms_ready")
        y_inv = sem("y_inv_ready")
        y_spread = sem("y_spread")
        y_final = sem("y_final")
        yhi_ready = sem("yhi_ready")
        y_split = sem("y_split")

        def psum_pair(j):
            return pw[:, 2 * (j % 2):2 * (j % 2) + 2, :]

        def bc(ap, n):
            return ap.unsqueeze(1).broadcast_to((ap.shape[0], n, ap.shape[1]))

        FFN_STEPS = 11
        ffn_base, norm_no, n = {}, {}, 0
        for name in phases:
            if name.startswith("in"):
                ffn_base[name] = n
                n += FFN_STEPS
        state = 0
        splits_before = {}
        splits = X_PAIRS
        state_of = {}
        for name in phases:
            if name == "in2":
                splits += X_PAIRS
            state_of[name] = state
            splits_before[name] = splits
            if name.startswith("out") or name in ("sout", "wo"):
                state += 1
                splits += X_PAIRS

        def gain_after(name):
            return {"start": G["ffn1"], "out0": G["mixer"], "sout": G["ffn2"], "out1": G["kv"],
                    "kv": G["ffn1"] + 8, "out2": G["mixer"] + 8, "wo": G["ffn2"] + 8,
                    "out3": G["final"]}[name]


        def load_unit(sp, n, j, source, dest=None):
            if not (isinstance(n, int) and n < SLOTS):
                sp.wait_ge(lo_ready, n - SLOTS + 1)
            sp.dma_start(raw[j][:, :] if dest is None else dest, source).then_inc(unit_loaded[j], 16)

        def split_hi(act, n, j, width=UK * 256):
            act.wait_ge(unit_loaded[j], ((n - j) // SLOTS + 1) * 16 if isinstance(n, int) else n)
            return act

        class Units:

            def __init__(self, n0, body, per):
                self.n0, self.body, self.per = n0, body, per

            def slot(self, u):
                return (self.n0 + u) % SLOTS

            def number(self, u):
                return self.body * self.per + (self.n0 + u)

            def loads(self, u):
                return self.body * (16 * self.per // SLOTS) + 16 * ((self.n0 + u) // SLOTS + 1)

        def hi(act, units, u):
            if isinstance(units.body, int) and units.number(u) >= n_units:
                return
            j = units.slot(u)
            act.wait_ge(unit_loaded[j], units.loads(u))
            if not (isinstance(units.body, int) and units.number(u) < SLOTS):
                act.wait_ge(unit_used, units.number(u) - SLOTS + 1)
            act.activation(whi[j][:, :], raw[j][:, :], ACT.Copy).then_inc(hi_ready, 1)

        def lo(dve, units, u):
            if isinstance(units.body, int) and units.number(u) >= n_units:
                return
            j = units.slot(u)
            dve.wait_ge(hi_ready, units.number(u) + 1)
            dve.tensor_tensor(wlo[j][:, :], raw[j][:, :], whi[j][:, :].bitcast(F32),
                              ALU.subtract).then_inc(lo_ready, 1)

        def products(pe, units, u, out, views, last_of_pair, x_hi, x_lo, wait=True):
            j = units.slot(u)
            pe.wait_ge(lo_ready, units.number(u) + 1)
            for o, ks in views:
                for c, (k, first, w0, last_k) in enumerate(ks):
                    wh, wl = whi[j][:, w0:w0 + P], wlo[j][:, w0:w0 + P]
                    pe.matmul(out[:, o, :], wh, x_hi[:, k, :], start=first, stop=False)
                    pe.matmul(out[:, o, :], wh, x_lo[:, k, :], start=False, stop=False)
                    last = pe.matmul(out[:, o, :], wl, x_hi[:, k, :], start=False, stop=last_k)
            last.then_inc(unit_used, 1)

        def k_views(k0, nk, n_k):
            return [(o, [(k0 + kk, k0 + kk == 0, kk * 256 + o * P, k0 + kk == n_k - 1)
                         for kk in range(nk)]) for o in range(2)]

        def row_unit(w, k0, nk, c0):
            return w.rearrange("(k p) c -> p k c", p=P)[:, k0:k0 + nk, bass.ds(c0, 256)]

        def in_pairs(pe, name, i, q0, n0, stat=False):
            units = Units(n0, i, 4)
            for r in range(2):
                pe.wait_ge(pair_free, i * 2 + (q0 + r - 1))
                for u in range(2):
                    if stat and r == 0:
                        pe.wait_ge(x_split, splits_before[name] - X_PAIRS + 2 * u + 2)
                    products(pe, units, 2 * r + u, psum_pair(r), k_views(4 * u, 4, KD), u == 1,
                             xh, xl)
                    if stat and r == 0 and name != "in2":
                        (stats, spread_stats)[u](pe, state_of[name])

        def stats(pe, state):
            pe.wait_ge(const_made, 3)
            pe.wait_ge(summed, X_PAIRS * (state + 1))
            token_sums(pe, buf_b, stat_ready)

        def token_sums(pe, squares, done):
            for c in range(S // P):
                for o in range(2):
                    last = pe.matmul(pa[:, 3, c:c + 1], squares[:, o, c * P:(c + 1) * P],
                                     ones[:, 0:1], start=o == 0, stop=o == 1)
            last.then_inc(done, 1)

        def spread_rows(pe, column, done):
            for c in range(S // P):
                last = pe.matmul(pa[:, 3, c * P:(c + 1) * P],
                                 column[:, c:c + 1].broadcast_to((P, P)), ident[:, :],
                                 start=True, stop=True)
            last.then_inc(done, 1)

        def spread_stats(pe, state):
            pe.wait_ge(inv_ready, state + 1)
            spread_rows(pe, inv_tok, spread_ready)

        def rms_act(act, state):
            act.wait_ge(stat_ready, state + 1)
            act.activation(rms_tok[:, :], pa[:, 3, 0:S // P], ACT.Sqrt, bias=eps_col[:, :],
                           scale=1.0 / D).then_inc(rms_ready, 1)

        def rstd_dve(dve, state):
            dve.wait_ge(rms_ready, state + 1)
            dve.reciprocal(inv_tok[:, :], rms_tok[:, :]).then_inc(inv_ready, 1)
            dve.wait_ge(spread_ready, state + 1)
            dve.tensor_copy(rstd[:, :], pa[:, 3, :]).then_inc(rstd_ready, 1)
            dve.wait_ge(rstd_ready, state + 1)

        def split_x(dve, m, p, gain, reads_done):
            for o in range(2):
                k = 2 * p + o
                g = gains[:, gain + k:gain + k + 1] if isinstance(k, int) else \
                    gains[:, bass.ds(k + gain, 1)]
                xs = x[:, k, :] if isinstance(k, int) else x[:, bass.ds(k, 1), :].squeeze(1)
                h = xh[:, k, :] if isinstance(k, int) else xh[:, bass.ds(k, 1), :].squeeze(1)
                l = xl[:, k, :] if isinstance(k, int) else xl[:, bass.ds(k, 1), :].squeeze(1)
                dve.tensor_scalar(h, xs, g, None, ALU.mult).then_inc(x_hi_ready, 1)
                dve.wait_ge(x_hi_ready, (m + p) * 2 + (o + 1))
                ins = dve.scalar_tensor_tensor(l, xs, g, h.bitcast(F32), ALU.mult, ALU.subtract)
            ins.then_inc(x_split, 1)

        def sq_act(act, state, p, q):
            act.wait_ge(pair_free, q + 1)
            act.wait_ge(summed, state * X_PAIRS + p)
            xs = x[:, 2 * p:2 * p + 2, :] if isinstance(p, int) else x[:, bass.ds(p * 2, 2), :]
            act.activation(buf_a[:, :, :], xs, ACT.Square).then_inc(squared, 1)

        def sum_pool(pool, state, p):
            pool.wait_ge(squared, state * X_PAIRS + p + 1)
            pool.tensor_tensor(buf_b[:, :, :], buf_b[:, :, :], buf_a[:, :, :],
                               ALU.add).then_inc(summed, 1)

        def out_dve(dve, name, scale, gain):
            n0, q0, pairs, per = at[name]
            m = splits_before[name]

            def body(i):
                units = Units(n0, i, 2 * per)
                for r in range(2):
                    for u in range(per):
                        lo(dve, units, r * per + u + LEAD)
                    dve.wait_ge(unit_used, units.number((r + 1) * per))
                    p = i * 2 + r
                    xs = x[:, 2 * p:2 * p + 2, :] if isinstance(p, int) else x[:, bass.ds(p * 2, 2), :]
                    dve.scalar_tensor_tensor(xs, psum_pair(r), scale, xs, ALU.mult, ALU.add)\
                        .then_inc(pair_free, 1)
                    dve.wait_ge(pair_free, p + (q0 + 1))
                    split_x(dve, m, p, gain, None)
            if name == last:
                for i in range(2):
                    body(i)
            else:
                with dve.Fori(0, 2) as i:
                    body(i)

        def out_act(act, name):
            n0, q0, pairs, per = at[name]

            def body(i):
                units = Units(n0, i, 2 * per)
                for r in range(2):
                    for u in range(per):
                        hi(act, units, r * per + u + LEAD)
                    sq_act(act, state_of[name] + 1, i * 2 + r, i * 2 + (q0 + r))
            if name == last:
                for i in range(2):
                    body(i)
            else:
                with act.Fori(0, 2) as i:
                    body(i)

        def out_pool(pool, name):
            state = state_of[name] + 1
            done = [v + FFN_STEPS for k, v in ffn_base.items() if phases.index(k) < phases.index(name)]
            if name == "sout":
                pool.wait_ge(y_final, GROUPS)
            if name == "wo":
                pool.wait_ge(heads_ready, 12)
            pool.wait_ge(hid_ready, max(done))
            pool.memset(buf_b[:, :, :], 0.0).then_inc(sum_cleared, 1)
            pool.wait_ge(sum_cleared, state + 1)
            with pool.Fori(0, X_PAIRS) as p:
                sum_pool(pool, state, p)

        def out_pe(pe, name, n_k, v_hi, v_lo, ready):
            n0, q0, pairs, per = at[name]
            with pe.Fori(0, 2) as i:
                units = Units(n0, i, 2 * per)
                for r in range(2):
                    pe.wait_ge(pair_free, i * 2 + (q0 + r - 1))
                    for u in range(per):
                        if r == 0:
                            ready(u)
                        products(pe, units, r * per + u, psum_pair(r),
                                 k_views(UK * u, min(UK, n_k - UK * u), n_k), u == per - 1, v_hi, v_lo)

        def out_sp(sp, name, w, n_k, between=None):
            n0, q0, pairs, per = at[name]

            def body(i):
                units = Units(n0, i, 2 * per)
                for r in range(2):
                    for u in range(per):
                        nk = min(UK, n_k - UK * u)
                        load(sp, units, r * per + u, row_unit(w, UK * u, nk, i * 512 + r * 256), nk)
            if between is not None:
                body(0)
                between()
                body(1)
                return
            with sp.Fori(0, 2) as i:
                body(i)

        def load(sp, units, u, source, nk=UK, wide=256):
            j = units.slot(u)
            if not (isinstance(units.body, int) and units.number(u) < SLOTS):
                sp.wait_ge(lo_ready, units.number(u) - SLOTS + 1)
            dest = raw[j][:, 0:nk * 256].rearrange("p (k c) -> p k c", c=wide)
            sp.dma_start(dest, source).then_inc(unit_loaded[j], 16)

        def ffn_in_sp(sp, name, w):
            n0, q0, pairs, per = at[name]

            def body(i):
                units = Units(n0, i, 4)
                for r in range(2):
                    for u in range(2):
                        load(sp, units, 2 * r + u, row_unit(w, UK * u, UK, i * 256 + r * F))
            ffn_steps(sp, n0, body)

        def ffn_in_pe(pe, name):
            n0, q0, pairs, per = at[name]
            in_pairs(pe, name, 0, q0, n0, stat=True)
            with pe.Fori(1, FFN_STEPS) as i:
                in_pairs(pe, name, i, q0, n0)

        def ffn_in_act(act, name):
            n0, q0, pairs, per = at[name]
            f0 = ffn_base[name]
            if name != "in2":
                rms_act(act, state_of[name])

            def body(i):
                units = Units(n0, i, 4)
                hi(act, units, LEAD)
                hi(act, units, LEAD + 1)
                act.wait_ge(pair_free, i * 2 + (q0 + 1))
                act.activation(buf_a[:, :, :], buf_a[:, :, :], ACT.Silu).then_inc(silu_done, 1)
                hi(act, units, LEAD + 2)
                hi(act, units, LEAD + 3)
            ffn_steps(act, n0, body)

        def ffn_steps(eng, n0, body):
            if n0 == 0:
                body(0)
            with eng.Fori(0 if n0 else 1, FFN_STEPS) as i:
                body(i)

        def ffn_in_dve(dve, name):
            n0, q0, pairs, per = at[name]
            f0 = ffn_base[name]
            if name != "in2":
                rstd_dve(dve, state_of[name])

            def body(i):
                units = Units(n0, i, 4)
                lo(dve, units, LEAD)
                lo(dve, units, LEAD + 1)
                dve.wait_ge(unit_used, units.number(2))
                dve.tensor_tensor(buf_a[:, :, :], psum_pair(0), bc(rstd[:, :], 2), ALU.mult)\
                    .then_inc(pair_free, 1)
                lo(dve, units, LEAD + 2)
                lo(dve, units, LEAD + 3)
                dve.wait_ge(unit_used, units.number(4))
                dve.tensor_tensor(buf_b[:, :, :], psum_pair(1), bc(rstd[:, :], 2), ALU.mult)\
                    .then_inc(pair_free, 1)
                dve.wait_ge(pair_free, i * 2 + (q0 + 2))
                dve.wait_ge(silu_done, i + (f0 + 1))
                dve.tensor_tensor(buf_b[:, :, :], buf_b[:, :, :], buf_a[:, :, :], ALU.mult)\
                    .then_inc(hid_made, 1)
                dve.wait_ge(hid_made, i + (f0 + 1))
                two = slice(0, 2) if isinstance(i, int) else bass.ds(i * 2, 2)
                h, l = hh[:, two, :], hl[:, two, :]
                dve.tensor_copy(h, buf_b[:, :, :]).then_inc(hid_hi, 1)
                dve.wait_ge(hid_hi, i + (f0 + 1))
                dve.tensor_tensor(l, buf_b[:, :, :], h.bitcast(F32), ALU.subtract)\
                    .then_inc(hid_ready, 1)
            ffn_steps(dve, n0, body)

        def ffn_out_ready(pe, name):
            f0 = ffn_base["in" + name[3:]]

            def ready(u):
                need = min(2 * u + 2, FFN_STEPS)
                pe.wait_ge(hid_ready, f0 + need)
            return ready

        eps_col = rest.tile("eps_col", [P, 1])

        w_ssm = t["ssm_w_in"][0]

        class Slot:

            def __init__(self, i, s0):
                self.i, self.s0, self.par = i, s0, s0 % 2
                self.units = Units(at["ssm"][0] + 6 * s0, i, 12) if "ssm" in at else None

            def count(self, k=0):
                return self.i * 2 + (self.s0 + k)

            def pairs(self, k):
                return self.i * 6 + (at["ssm"][1] + 3 * self.s0 + k)

            def first(self, k):
                return isinstance(self.i, int) and self.s0 - k < 0

        def slots(eng, slot):
            slot(Slot(0, 0))
            slot(Slot(0, 1))
            with eng.Fori(0, 3) as i:
                slot(Slot(i, 2))
                slot(Slot(i, 3))
            slot(Slot(0, 8))
            slot(Slot(0, 9))

        def has(s, k):
            return not isinstance(s.i, int) or 0 <= s.s0 - k < GROUPS

        def ssm_pe(pe):
            n0, q0, _, _ = at["ssm"]

            def unit(s, u):
                if not has(s, 0):
                    return
                if u % 2 == 0:
                    pe.wait_ge(pair_free, s.pairs(u // 2 - 1))
                j = (3 * s.s0 + u // 2) % 2
                if u < 4:
                    if isinstance(s.i, int) and s.s0 == 0 and u < 2:
                        pe.wait_ge(x_split, splits_before["ssm"] - X_PAIRS + 2 * u + 2)
                    products(pe, s.units, u, psum_pair(j), k_views(4 * (u % 2), 4, KD), u % 2 == 1,
                             xh, xl)
                else:
                    views = [(u - 4, [(k, k == 0, k * P, k == KD - 1) for k in range(KD)])]
                    products(pe, s.units, u, psum_pair(j), views, u == 5, xh, xl)

            def dt_product():
                pe.wait_ge(wdt_ready, 1)
                for k in range(KD):
                    pe.matmul(pa[:, 2, :], wdt_hi[:, k, :], xh[:, k, :], start=k == 0, stop=False)
                    pe.matmul(pa[:, 2, :], wdt_hi[:, k, :], xl[:, k, :], start=False, stop=False)
                    l = pe.matmul(pa[:, 2, :], wdt_lo[:, k, :], xh[:, k, :], start=False, stop=k == KD - 1)
                l.then_inc(dt_used, 1)

            def dt_turn():
                pe.wait_ge(cum_ready, 1)
                idn = ident[DT0:P, DT0:P]
                for c in range(NC):
                    for v, src in ((0, dt_c), (1, dt_t)):
                        l = pe.transpose(pa[:, 2, (v * NC + c) * HEADS:(v * NC + c + 1) * HEADS],
                                         src[DT0:P, c * L:(c + 1) * L], idn)
                l.then_inc(tok_turned, 1)

            def part_a(s):
                pe.wait_ge(conv_done, s.count())
                if not s.first(2):
                    pe.wait_ge(y_gated, s.count(-1))
                    pe.wait_ge(y_final, s.count(-1))
                for c in range(NC):
                    for j in range(2):
                        o = (c % 2) * 256 + j * P
                        pe.transpose(pa[:, c // 2, o:o + P], xbc[:, j, c * L:(c + 1) * L], ident[:, :])
                for c in range(NC):
                    l = pe.transpose(pa[:, 2, c * P:(c + 1) * P], xbc[:, 2, c * L:(c + 1) * L],
                                     ident[:, :])
                l.then_inc(turned_a, 1)
                for c in range(NC):
                    l = pe.matmul(pa[:, 3, c * L:(c + 1) * L], xbc[:, 2, c * L:(c + 1) * L],
                                  xbc[:, 3, c * L:(c + 1) * L], start=True, stop=True)
                l.then_inc(cb_product, 1)

            def part_b(s):
                pe.wait_ge(xde_ready, s.count())
                pe.wait_ge(btok_ready, s.count())
                pe.wait_ge(cbm_ready, s.count())
                for c in range(NC - 1):
                    o = (c % 2) * 256
                    l = pe.matmul(pa[:, 2 + c // 2, o:o + 256], btok[:, c, :], xde[:, c, :],
                                  start=True, stop=True)
                l.then_inc(states_product, 1)

            def part_c(s):
                pe.wait_ge(m_ready, s.count())
                pe.wait_ge(c_ready, s.count())
                pe.wait_ge(xdt_ready, s.count())
                pe.wait_ge(prev_step, s.count() * 5)
                for h in range(HG):
                    for c in range(NC):
                        out = pa[64 * (h % 2):64 * (h % 2) + HP, h // 2, c * L:(c + 1) * L]
                        l = pe.matmul(out, xdt[:, c, h * HP:(h + 1) * HP], segm[:, h, c * L:(c + 1) * L],
                                      start=True, stop=c == 0)
                        if c:
                            l = pe.matmul(out, prev[:, c - 1, h * HP:(h + 1) * HP],
                                          cumb[:, h, c * L:(c + 1) * L], start=False, stop=True)
                l.then_inc(y_product, 1)

            def slot(s):
                unit(s, 0)
                if isinstance(s.i, int) and s.s0 == 0:
                    stats(pe, state_of["ssm"])
                if has(s, 2):
                    pe.wait_ge(y_squared, s.count(-1))
                    token_sums(pe, ysq, y_stat)
                unit(s, 1)
                if isinstance(s.i, int) and s.s0 == 0:
                    spread_stats(pe, state_of["ssm"])
                if has(s, 2):
                    pe.wait_ge(y_inv, s.count(-1))
                    spread_rows(pe, yinv, y_spread)
                unit(s, 2)
                if isinstance(s.i, int) and s.s0 == 0:
                    dt_product()
                if has(s, 1):
                    part_a(s)
                unit(s, 3)
                unit(s, 4)
                if isinstance(s.i, int) and s.s0 == 0:
                    dt_turn()
                if has(s, 1):
                    part_b(s)
                unit(s, 5)
                if has(s, 1):
                    part_c(s)
            slots(pe, slot)

        def ssm_act(act):
            n0 = at["ssm"][0]
            act.wait_ge(unit_used, n0)
            act.dma_start(wdt[:, :, :], w_ssm.rearrange("(k p) c -> p k c", p=P)[:, :, 6176 - P:6176])\
                .then_inc(wdt_loaded, 16)
            d = slice(DT0, P)

            def dt_steps():
                act.wait_ge(dt_v, 1)
                act.activation(dt_e[d, :], dt_raw[d, :], ACT.Abs).then_inc(dt_s, 1)
                act.wait_ge(dt_s, 1)
                act.wait_ge(ssm_consts, 16 * 4)
                act.activation(dt_e[d, :], dt_e[d, :], ACT.Exp, scale=-1.0).then_inc(dt_s, 1)
                act.activation(a_neg[d, :], a_neg[d, :], ACT.Exp).then_inc(dt_s, 1)
                act.wait_ge(dt_v, 2)
                act.activation(dt_ln[d, :], dt_u[d, :], ACT.Ln).then_inc(dt_s, 1)

            def slot(s):
                if has(s, 1):
                    act.wait_ge(cum_stored, 16)
                    if isinstance(s.i, int) and s.s0 == 1:
                        act.wait_ge(tok_ready, 1)
                    if not s.first(2):
                        act.wait_ge(y_product, s.count(-1))
                    g = s.count(-1)
                    rows = cum_dram[bass.ds(g * HG, HG), :]
                    act.dma_start(cumb[:, :, :], rows.partition_broadcast(P)).then_inc(cum_loaded, 16)
                if has(s, 0):
                    hi(act, s.units, LEAD)
                if isinstance(s.i, int) and s.s0 == 0:
                    rms_act(act, state_of["ssm"])
                if has(s, 2):
                    act.wait_ge(y_stat, s.count(-1))
                    act.activation(yrms[:, :], pa[:, 3, 0:NC], ACT.Sqrt, bias=eps_col[:, :],
                                   scale=1.0 / 256).then_inc(y_rms, 1)
                if has(s, 1):
                    for r in range(2):
                        act.wait_ge(params_ready, s.count() * 5)
                        for tt in range(2 * r, 2 * r + 2):
                            act.wait_ge(pair_free, s.pairs(0))
                            act.activation(xbc[:, tt, :], pre[:, tt, 3:3 + S], ACT.Identity,
                                           bias=gcw[1 - s.par][:, 4, tt:tt + 1],
                                           scale=gcw[1 - s.par][:, 3, tt:tt + 1]).then_inc(conv_base, 1)
                    if has(s, 0):
                        hi(act, s.units, LEAD + 1)
                    for r in range(2):
                        act.wait_ge(conv_tap, s.count(-1) * 12 + 6 * r + 6)
                        act.activation(tanh[:, 2 * r:2 * r + 2, :], xbc[:, 2 * r:2 * r + 2, :],
                                       ACT.Tanh).then_inc(conv_tanh, 1)
                elif has(s, 0):
                    hi(act, s.units, LEAD + 1)
                if has(s, 0):
                    act.wait_ge(pair_free, s.pairs(1))
                    zb = (buf_a, buf_b)[s.par]
                    act.activation(ztanh(s)[:, :, :], zb[:, :, :], ACT.Tanh, scale=0.5).then_inc(z_tanh, 1)
                    hi(act, s.units, LEAD + 2)
                    hi(act, s.units, LEAD + 3)
                if isinstance(s.i, int) and s.s0 == 0:
                    act.wait_ge(wdt_loaded, 16)
                    act.activation(wdt_hi[:, :, :], wdt[:, :, :], ACT.Copy).then_inc(wdt_hi_ready, 1)
                    dt_steps()
                if has(s, 1):
                    act.wait_ge(turned_a, s.count())
                    act.activation(btok[:, :, :], pa[:, 2, :], ACT.Copy).then_inc(btok_ready, 1)
                    act.wait_ge(dte_diff, s.count())
                    act.activation(dte[:, :, :], dte[:, :, :], ACT.Exp).then_inc(dte_ready, 1)
                    act.wait_ge(seg_ready, s.count() * 16)
                    act.activation(segm[:, :, :], segm[:, :, :], ACT.Exp).then_inc(decay_ready, 1)
                    act.activation(cumb[:, :, :], cumb[:, :, :], ACT.Exp).then_inc(growth_ready, 1)
                if has(s, 0):
                    hi(act, s.units, LEAD + 4)
                    hi(act, s.units, LEAD + 5)
                if isinstance(s.i, int) and s.s0 == 0:
                    act.wait_ge(cum_ready, 1)
                    act.dma_start(cum_dram, dt_c[DT0:P, :]).then_inc(cum_stored, 16)
                if has(s, 1):
                    act.wait_ge(y_gated, s.count())
                    g = s.count(-1)
                    act.activation(ysq[:, :, :], y32[:, bass.ds(g * 2, 2), :], ACT.Square)\
                        .then_inc(y_squared, 1)
            slots(act, slot)
            for u in range(4):
                act.wait_ge(y_final, min(2 * u + 2, GROUPS) if u else GROUPS)
                act.activation(y_hi[:, 4 * u:4 * u + 4, :], y32[:, 4 * u:4 * u + 4, :], ACT.Copy)\
                    .then_inc(yhi_ready, 1)

        def ztanh(s):
            return tanh_z

        def ssm_dve(dve):
            n0, q0, _, _ = at["ssm"]
            d = slice(DT0, P)

            def dt_steps():
                dve.wait_ge(wdt_hi_ready, 1)
                dve.tensor_tensor(wdt_lo[:, :, :], wdt[:, :, :], wdt_hi[:, :, :].bitcast(F32),
                                  ALU.subtract).then_inc(wdt_ready, 1)
                dve.wait_ge(dt_used, 1)
                dve.tensor_tensor(dt_raw[d, :], pa[d, 2, :], rstd[d, :], ALU.mult).then_inc(cum_ready_v, 1)
                dve.wait_ge(cum_ready_v, 1)
                dve.wait_ge(ssm_consts, 16 * 4)
                dve.tensor_scalar(dt_raw[d, :], dt_raw[d, :], dt_bias[d, :], None, ALU.add).then_inc(dt_v, 1)
                dve.wait_ge(dt_s, 2)
                dve.tensor_scalar(dt_u[d, :], dt_e[d, :], 1.0, None, ALU.add).then_inc(dt_v, 1)
                dve.wait_ge(dt_v, 2)
                dve.reciprocal(dt_r[d, :], dt_u[d, :]).then_inc(dt_v, 1)
                dve.scalar_tensor_tensor(dt_t[d, :], dt_u[d, :], 1.0, dt_e[d, :], ALU.subtract,
                                         ALU.subtract).then_inc(dt_v, 1)
                dve.wait_ge(dt_v, 4)
                dve.scalar_tensor_tensor(dt_c[d, :], dt_t[d, :], -1.0, dt_r[d, :], ALU.mult,
                                         ALU.mult).then_inc(dt_v, 1)
                dve.wait_ge(dt_v, 5)
                dve.wait_ge(dt_s, 4)
                dve.tensor_tensor(dt_u[d, :], dt_c[d, :], dt_ln[d, :], ALU.add).then_inc(dt_v, 1)
                dve.wait_ge(dt_v, 6)
                dve.scalar_tensor_tensor(dt_t[d, :], dt_raw[d, :], 0.0, dt_u[d, :], ALU.max,
                                         ALU.add).then_inc(dt_v, 1)
                dve.wait_ge(dt_v, 7)
                dve.tensor_scalar(dt_r[d, :], dt_t[d, :], a_neg[d, :], -1.0, ALU.mult, ALU.mult)\
                    .then_inc(dt_v, 1)
                dve.wait_ge(dt_v, 8)
                for c in range(NC):
                    l = dve.tensor_tensor_scan(dt_c[d, c * L:(c + 1) * L], ones[d, :],
                                               dt_r[d, c * L:(c + 1) * L], 0.0, ALU.mult, ALU.add)
                l.then_inc(cum_ready, 1)
                dve.wait_ge(tok_turned, 1)
                dve.tensor_copy(tok_all[:, :, :, :], pa[:, 2, 0:2 * NC * HEADS]).then_inc(tok_ready, 1)
                dve.wait_ge(tok_ready, 1)

            def conv(s, r):
                for k in (2, 1, 0):
                    for tt in (2 * r, 2 * r + 1):
                        dve.wait_ge(conv_base, s.count(-1) * 4 + (tt + 1))
                        if k < 2:
                            dve.wait_ge(conv_tap, s.count(-1) * 12 + (6 * r + 2 * (1 - k) + (tt - 2 * r) + 1))
                        dve.scalar_tensor_tensor(xbc[:, tt, :], pre[:, tt, k:k + S],
                                                 gcw[1 - s.par][:, k, tt:tt + 1], xbc[:, tt, :],
                                                 ALU.mult, ALU.add).then_inc(conv_tap, 1)

            def silu(s, r):
                dve.wait_ge(conv_tanh, s.count(-1) * 2 + (r + 1))
                v = xbc[:, 2 * r:2 * r + 2, :]
                ins = dve.scalar_tensor_tensor(v, tanh[:, 2 * r:2 * r + 2, :], 1.0, v, ALU.add, ALU.mult)
                if r:
                    ins.then_inc(conv_done, 1)

            def slot(s):
                if has(s, 1):
                    dve.wait_ge(unit_used, s.units.number(0))
                    dve.tensor_tensor(pre[:, 2:4, 3:3 + S], psum_pair(3 * s.s0 - 1), bc(rstd[:, :], 2),
                                      ALU.mult).then_inc(pair_free, 1)
                if has(s, 0):
                    lo(dve, s.units, LEAD)
                if isinstance(s.i, int) and s.s0 == 0:
                    rstd_dve(dve, state_of["ssm"])
                if has(s, 1):
                    conv(s, 0)
                if has(s, 2):
                    dve.wait_ge(y_rms, s.count(-1))
                    dve.reciprocal(yinv[:, :], yrms[:, :]).then_inc(y_inv, 1)
                if has(s, 0):
                    lo(dve, s.units, LEAD + 1)
                if has(s, 1):
                    conv(s, 1)
                    silu(s, 0)
                if has(s, 2):
                    dve.wait_ge(y_spread, s.count(-1))
                    for j in range(2):
                        yt = y32[:, bass.ds(s.count(-2) * 2 + j, 1), :].squeeze(1)
                        ins = dve.scalar_tensor_tensor(yt, yt, gdn[s.par][:, 1, j:j + 1], pa[:, 3, :],
                                                       ALU.mult, ALU.mult)
                    ins.then_inc(y_final, 1)
                if has(s, 1):
                    silu(s, 1)
                if has(s, 0):
                    zb = (buf_a, buf_b)[s.par]
                    dve.wait_ge(unit_used, s.units.number(2))
                    dve.tensor_tensor(zb[:, :, :], psum_pair(3 * s.s0), bc(rstd[:, :], 2), ALU.mult)\
                        .then_inc(pair_free, 1)
                    lo(dve, s.units, LEAD + 2)
                    lo(dve, s.units, LEAD + 3)
                    dve.wait_ge(z_tanh, s.count(1))
                    dve.scalar_tensor_tensor(zb[:, :, :], tanh_z[:, :, :], 1.0, zb[:, :, :], ALU.add,
                                             ALU.mult).then_inc(z_ready, 1)
                if isinstance(s.i, int) and s.s0 == 0:
                    dt_steps()
                if has(s, 1):
                    g = s.count(-1)
                    dve.tensor_copy(gtok[:, :, :, :], tok_all[:, :, :, bass.ds(g * HG, HG)])\
                        .then_inc(gtok_ready, 1)
                    dve.wait_ge(gtok_ready, s.count())
                    dve.wait_ge(turned_a, s.count())
                    heads = pa[:, 0:2, :].rearrange("p b (c p2) -> p (b c p2)", c=8)
                    dve.tensor_tensor(
                        xdt[:, :, :].rearrange("p c (h q) -> p (c h) q", h=HG),
                        pa[:, 0:2, :].rearrange("p b (m q) -> p (b m) q", q=HP),
                        gtok[:, 1, :, :].rearrange("p c h -> p (c h)").unsqueeze(2)
                        .broadcast_to((P, NC * HG, HP)), ALU.mult).then_inc(xdt_ready, 1)
                    dve.wait_ge(cum_loaded, s.count() * 16)
                    ends = cumb[:, :, :].rearrange("p h (c l) -> p c h l", l=L)[:, :, :, L - 1]
                    dve.tensor_tensor(dte[:, :, :], ends, gtok[:, 0, :, :], ALU.subtract)\
                        .then_inc(dte_diff, 1)
                    for h in range(HG):
                        for c in range(NC):
                            dve.tensor_scalar(segm[:, h, c * L:(c + 1) * L],
                                              cumb[:, h, c * L:(c + 1) * L],
                                              gtok[:, 0, c, h:h + 1], 0.0, ALU.subtract, ALU.min)\
                                .then_inc(seg_ready, 1)
                    dve.wait_ge(cb_product, s.count())
                    dve.tensor_tensor(cbm[:, :].rearrange("p (c l) -> p c l", c=NC),
                                      pa[:, 3, :].rearrange("p (c l) -> p c l", c=NC),
                                      bc(mask[:, :], NC), ALU.mult).then_inc(cbm_ready, 1)
                    dve.wait_ge(dte_ready, s.count())
                    dve.wait_ge(xdt_ready, s.count())
                    dve.tensor_tensor(
                        xde[:, :, :].rearrange("p c (h q) -> p (c h) q", h=HG),
                        xdt[:, :, :].rearrange("p c (h q) -> p (c h) q", h=HG),
                        dte[:, :, :].rearrange("p c h -> p (c h)").unsqueeze(2)
                        .broadcast_to((P, NC * HG, HP)), ALU.mult).then_inc(xde_ready, 1)
                if has(s, 0):
                    dve.wait_ge(unit_used, s.units.number(4))
                    dve.tensor_tensor(pre[:, 0:2, 3:3 + S], psum_pair(3 * s.s0 + 1), bc(rstd[:, :], 2),
                                      ALU.mult).then_inc(pair_free, 1)
                    lo(dve, s.units, LEAD + 4)
                if has(s, 1):
                    dve.wait_ge(decay_ready, s.count())
                    dve.wait_ge(cbm_ready, s.count())
                    dve.tensor_tensor(segm[:, :, :], segm[:, :, :], bc(cbm[:, :], HG), ALU.mult)\
                        .then_inc(m_ready, 1)
                    dve.wait_ge(growth_ready, s.count())
                    dve.tensor_copy(cd[:, :, :], cumb[:, :, :].rearrange("p h (c l) -> p h c l", l=L)
                                    [:, :, :, L - 1]).then_inc(cd_ready, 1)
                    dve.wait_ge(cd_ready, s.count())
                    dve.tensor_tensor(cumb[:, :, :], cumb[:, :, :], bc(xbc[:, 3, :], HG), ALU.mult)\
                        .then_inc(c_ready, 1)
                    dve.wait_ge(states_product, s.count())
                    step = 0
                    for c in range(NC - 1):
                        src = pa[:, 2 + c // 2, (c % 2) * 256:(c % 2) * 256 + 256]
                        if c == 0:
                            dve.tensor_copy(prev[:, 0, :], src).then_inc(prev_step, 1)
                            step += 1
                            continue
                        dve.wait_ge(prev_step, s.count(-1) * 5 + step)
                        dve.tensor_tensor(prev[:, c, :].rearrange("p (h q) -> p h q", h=HG),
                                          prev[:, c - 1, :].rearrange("p (h q) -> p h q", h=HG),
                                          cd[:, :, c:c + 1].broadcast_to((P, HG, HP)), ALU.mult)\
                            .then_inc(prev_step, 1)
                        step += 1
                        dve.wait_ge(prev_step, s.count(-1) * 5 + step)
                        dve.tensor_tensor(prev[:, c, :], prev[:, c, :], src, ALU.add)\
                            .then_inc(prev_step, 1)
                        step += 1
                if has(s, 0):
                    lo(dve, s.units, LEAD + 5)
                if has(s, 1):
                    dve.wait_ge(y_product, s.count())
                    dn = gdn[1 - s.par]
                    for j in range(2):
                        yt = y32[:, bass.ds(s.count(-1) * 2 + j, 1), :].squeeze(1)
                        dve.scalar_tensor_tensor(yt, xbc[:, j, :], dn[:, 0, j:j + 1], pa[:, j, :],
                                                 ALU.mult, ALU.add).then_inc(y_plus, 1)
                    dve.wait_ge(y_plus, s.count() * 2)
                    yp = y32[:, bass.ds(s.count(-1) * 2, 2), :]
                    zb = (buf_a, buf_b)[1 - s.par]
                    dve.scalar_tensor_tensor(yp, yp, 0.5, zb[:, :, :], ALU.mult, ALU.mult)\
                        .then_inc(y_gated, 1)
            slots(dve, slot)
            for u in range(4):
                dve.wait_ge(yhi_ready, u + 1)
                dve.tensor_tensor(y_lo[:, 4 * u:4 * u + 4, :], y32[:, 4 * u:4 * u + 4, :],
                                  y_hi[:, 4 * u:4 * u + 4, :].bitcast(F32), ALU.subtract)\
                    .then_inc(y_split, 1)

        def ssm_pool(pool):
            n0 = at["ssm"][0]
            pool.wait_ge(unit_used, n0)
            pool.memset(pre[:, :, 0:3], 0.0).then_inc(halo_ready, 1)
            pool.wait_ge(cw_ready, 2)
            pool.wait_ge(gains_ready, 1)
            pool.wait_ge(ssm_consts, 16 * 4)

            def group(i, r):
                g = i * 2 + r
                if not isinstance(i, int) or i > 0:
                    pool.wait_ge(y_final, g - 1)
                for dst, src in ((gcw[r][:, :, 0:2], cw[:, :, bass.ds(g * 2, 2)]),
                                 (gcw[r][:, :, 2:3], cw[:, :, bass.ds(g + 16, 1)]),
                                 (gcw[r][:, :, 3:4], cw[:, :, bass.ds(g + 24, 1)]),
                                 (gdn[r][:, 0, :], dskip[:, bass.ds(g * 2, 2)]),
                                 (gdn[r][:, 1, :], gains[:, bass.ds(g * 2 + G["ssm_norm"], 2)])):
                    pool.tensor_copy(dst, src).then_inc(params_ready, 1)
            group(0, 0)
            group(0, 1)
            with pool.Fori(1, 4) as i:
                group(i, 0)
                group(i, 1)

        def ssm_sp(sp):
            def slot(s):
                if not has(s, 0):
                    return
                g = s.count()
                for u in range(4):
                    load(sp, s.units, u, row_unit(w_ssm, UK * (u % 2), UK, g * 256 + (u // 2) * DI))
                for u in range(2):
                    src = w_ssm.rearrange("(k p) c -> p k c", p=P)[
                        :, :, bass.ds(g * P + (2 * DI + u * GROUPS * NST), P)]
                    load(sp, s.units, 4 + u, src, wide=P)
            slots(sp, slot)


        class PairSlot:
            def __init__(self, name, i, s0):
                self.i, self.s0, self.name = i, s0, name
                self.n0, self.q0, self.pairs, _ = at[name]
                self.units = Units(self.n0 + 2 * s0, i, 4)
                self.turn = name == "kv" and s0 > 4
                self.work = not isinstance(i, int) or s0 < self.pairs
                self.before = 0 if name == "kv" else at["kv"][2]
                self.ropes_before = 0 if name == "kv" else 4

            def count(self, k=0):
                return self.i * 2 + (self.s0 + k)

            def done(self, k=0):
                return self.i * 2 + (self.s0 + self.before + k)

            def roped(self, k=0):
                return self.i * 2 + (self.s0 + self.ropes_before + k)

        def pair_slots(eng, name, slot):
            slot(PairSlot(name, 0, 0))
            if name == "kv":
                with eng.Fori(0, 2) as i:
                    slot(PairSlot(name, i, 1))
                    slot(PairSlot(name, i, 2))
                rest_of = range(5, 9)
            else:
                rest_of = range(1, 5)
            for s0 in rest_of:
                slot(PairSlot(name, 0, s0))

        def pair_pe(pe, name):
            def slot(s):
                par = s.s0 % 2
                for u in range(2):
                    if s.work:
                        if u == 0:
                            pe.wait_ge(pair_free, s.count(s.q0 - 1))
                        if s.s0 == 0:
                            pe.wait_ge(x_split, splits_before[name] - X_PAIRS + 2 * u + 2)
                        products(pe, s.units, u, psum_pair(par), k_views(4 * u, 4, KD), u == 1, xh, xl)
                    if s.s0 == 0:
                        (stats, spread_stats)[u](pe, state_of[name])
                    elif u == 0:
                        pe.wait_ge(pair_free, s.count(s.q0))
                        if name == "kv" and s.s0 == 1:
                            pe.wait_ge(rope_loaded, 16 * 3)
                        if name == "q" and s.s0 == 1:
                            pe.wait_ge(rope_loaded, 32 * 3)
                        if s.turn:
                            for c in range(NC):
                                for o in range(2):
                                    w0 = (c % 2) * 256 + o * P
                                    l = pe.transpose(pa[:, c // 2, w0:w0 + P],
                                                     buf_a[:, o, c * P:(c + 1) * P], ident[:, :])
                        else:
                            for o in range(2):
                                l = pe.matmul(pa[:, o, :], rot[:, :], buf_a[:, o, :], start=True, stop=True)
                        l.then_inc(head_rotated, 1)
            pair_slots(pe, name, slot)

        def pair_act(act, name):
            dram = q_dram if name == "q" else k_dram

            def slot(s):
                if s.work:
                    hi(act, s.units, LEAD)
                if s.s0 == 0:
                    if name == "kv":
                        for r in range(2):
                            act.sem_inc(heads_stored[r], 16)
                        act.wait_ge(unit_used, s.n0)
                    else:
                        act.wait_ge(unit_used, s.n0)
                    for dst, src in ((cos_t, t["rope_tables"][0]), (sin_t, t["rope_tables"][1]),
                                     (rot, t["rope_rotation"])):
                        act.dma_start(dst[:, :], src).then_inc(rope_loaded, 16)
                    rms_act(act, state_of[name])
                if s.work:
                    hi(act, s.units, LEAD + 1)
                if s.s0:
                    act.wait_ge(heads_ready, s.done())
                    d = v_dram if s.turn else dram
                    h0 = s.count(-1) * 2 - (8 if s.turn else 0)
                    par = (s.s0 - 1) % 2
                    act.dma_start(d[bass.ds(h0, 2)].rearrange("o p x -> p o x"),
                                  heads_out[par][:, :, :]).then_inc(heads_stored[par], 16)
            pair_slots(act, name, slot)

        def pair_dve(dve, name):
            def slot(s):
                if s.s0:
                    dve.wait_ge(unit_used, s.units.number(0))
                    dve.tensor_tensor(buf_a[:, :, :], psum_pair(s.s0 - 1), bc(rstd[:, :], 2), ALU.mult)\
                        .then_inc(pair_free, 1)
                if s.work:
                    lo(dve, s.units, LEAD)
                if s.s0 == 0:
                    rstd_dve(dve, state_of[name])
                    dve.wait_ge(rope_loaded, 16 * 3 * (2 if name == "q" else 1))
                if s.s0:
                    par = (s.s0 - 1) % 2
                    if not s.turn:
                        dve.wait_ge(pair_free, s.count(s.q0))
                        dve.tensor_tensor(buf_b[:, :, :], buf_a[:, :, :], bc(cos_t[:, :], 2), ALU.mult)\
                            .then_inc(rope_cos, 1)
                    if isinstance(s.i, int):
                        dve.wait_ge(heads_stored[par], 16 * ((s.done(-1) + 1 - par) // 2 + 1))
                    else:
                        dve.wait_ge(heads_stored[par], (s.i + 1) * 16)
                    dve.wait_ge(head_rotated, s.done())
                    if s.turn:
                        dve.tensor_copy(
                            heads_out[par][:, :, :].rearrange("p o (c e) -> p o c e", e=P),
                            pa[:, 0:2, :].rearrange("p b (c o e) -> p o (b c) e", c=2, o=2))\
                            .then_inc(heads_ready, 1)
                    else:
                        dve.tensor_tensor(heads_out[par][:, :, :], pa[:, 0:2, :], bc(sin_t[:, :], 2),
                                          ALU.mult).then_inc(rope_sin, 1)
                        dve.wait_ge(rope_sin, s.roped())
                        dve.tensor_tensor(heads_out[par][:, :, :], heads_out[par][:, :, :],
                                          buf_b[:, :, :], ALU.add).then_inc(heads_ready, 1)
                if s.work:
                    lo(dve, s.units, LEAD + 1)
            pair_slots(dve, name, slot)
            if name == "kv":
                for r in range(2):
                    dve.wait_ge(heads_stored[r], 16 * 5)
                for p in range(X_PAIRS):
                    split_x(dve, splits_before["in2"] - X_PAIRS, p, gain_after("kv"), None)

        def pair_sp(sp, name, w):
            n0, q0, pairs, _ = at[name]
            with sp.Fori(0, pairs // 2) as i:
                units = Units(n0, i, 4)
                for r in range(2):
                    for u in range(2):
                        load(sp, units, 2 * r + u, row_unit(w, UK * u, UK, i * 512 + r * 256))


        class Step:
            def __init__(self, i, u):
                self.i, self.u0, self.u = i, u, u % 8
                self.q = u % 4
                self.h = (u % 8) // 4
                self.n = (self.q + 1) * P
                self.par = u % 2
                self.last_q = self.q == 3

            def count(self, k=0):
                return self.i * 8 + (self.u0 + k)

            def head(self, k=0):
                return self.i * 2 + (self.u0 // 4 + k)

            def exists(self):
                return not isinstance(self.i, int) or 0 <= self.i * 8 + self.u0 < AH * NC

        def att_bodies(eng, body):
            body(0)
            with eng.Fori(1, 3) as i:
                body(i)
            body(3)

        def att_pe(pe):
            def logits(s):
                if not s.exists():
                    return
                if s.q == 0:
                    pe.wait_ge(head_loaded[s.h], s.i * 48 + 48 * ((s.u0 // 8) + 1))
                if not (isinstance(s.i, int) and s.count() < 2):
                    pe.wait_ge(exp_ready, s.count(-1) * 2)
                for m in range(2):
                    d = slice(m * HP, (m + 1) * HP)
                    l = pe.matmul(pw[:, 2 * s.par + m, 0:s.n], q_cur[s.h][d, s.q * P:(s.q + 1) * P],
                                  k_cur[s.h][d, 0:s.n], start=True, stop=True)
                l.then_inc(logits_ready, 1)

            def turn(s):
                pe.wait_ge(w_ready, s.count(1))
                if not (isinstance(s.i, int) and s.count() < 2):
                    pe.wait_ge(wt_ready, s.count(-1))
                for b in range(s.q + 1):
                    l = pe.transpose(pa[:, s.par, b * P:(b + 1) * P], probs[s.par][:, 0, b * P:(b + 1) * P],
                                     ident[:, :])
                l.then_inc(w_turned, 1)

            def values(s):
                if not s.exists():
                    return
                pe.wait_ge(wt_ready, s.count(1))
                if s.q == 0 and not (isinstance(s.i, int) and s.head() < 2):
                    pe.wait_ge(o_copied, s.head(-1))
                for b in range(s.q + 1):
                    l = pe.matmul(pa[:, 2 + s.h, s.q * P:(s.q + 1) * P], v_cur[s.h][:, b, :],
                                  w_t[s.par][:, b * P:(b + 1) * P], start=b == 0, stop=b == s.q)
                l.then_inc(pv_done, 1)

            def body(i):
                if isinstance(i, int) and i == 0:
                    logits(Step(0, 0))
                    logits(Step(0, 1))
                for u in range(8):
                    logits(Step(i, u + 2))
                    turn(Step(i, u))
                    values(Step(i, u - 1))
            pe.wait_ge(pair_free, at["q"][1] + at["q"][2])
            pe.wait_ge(heads_ready, 12)
            att_bodies(pe, body)
            values(Step(3, 7))
            for h in range(AH):
                pe.wait_ge(o_squared, h + 1)
                for c in range(NC):
                    l = pe.matmul(pa[:, 0, h * NC + c:h * NC + c + 1], osq_of(h)[:, c * P:(c + 1) * P],
                                  ones[:, 0:1], start=True, stop=True)
                l.then_inc(o_summed, 1)
            pe.wait_ge(o_inv_ready, 1)
            for h in range(AH):
                if h >= 2:
                    pe.wait_ge(o_normed, h - 1)
                for c in range(NC):
                    l = pe.matmul(pa[:, 2 + h % 2, c * P:(c + 1) * P],
                                  oinv[:, h, c:c + 1].broadcast_to((P, P)), ident[:, :],
                                  start=True, stop=True)
                l.then_inc(o_spread, 1)

        def osq_of(h):
            return (q_cur[0], q_cur[1], k_cur[0], k_cur[1])[h % 4]

        def att_act(act):
            act.wait_ge(lam_step, 2)
            act.activation(lam_s[:, :], lam_s[:, :], ACT.Exp).then_inc(lam_exp, 1)

            def exps(s):
                if not s.exists():
                    return
                act.wait_ge(bias_ready, s.count(1))
                if not (isinstance(s.i, int) and s.count() < 2):
                    act.wait_ge(w_turned, s.count(-1))
                for m in range(2):
                    act.activation(probs[s.par][:, m, 0:s.n], pw[:, 2 * s.par + m, 0:s.n], ACT.Exp,
                                   bias=nb[s.par][:, m:m + 1], scale=SCALE,
                                   accum_out=rs[s.par][:, m:m + 1]).then_inc(exp_ready, 1)

            def copy_turned(s):
                act.wait_ge(w_turned, s.count(1))
                if not (isinstance(s.i, int) and s.count() < 2):
                    act.wait_ge(pv_done, s.count(-1))
                act.activation(w_t[s.par][:, 0:s.n], pa[:, s.par, 0:s.n], ACT.Copy).then_inc(wt_ready, 1)

            def copy_o(s):
                if not s.exists():
                    return
                act.wait_ge(pv_done, s.count(1))
                h = s.head()
                act.activation(o_all[:, bass.ds(h, 1), :].squeeze(1) if not isinstance(h, int) else
                               o_all[:, h, :], pa[:, 2 + s.h, :], ACT.Copy).then_inc(o_copied, 1)

            def body(i):
                if isinstance(i, int) and i == 0:
                    exps(Step(0, 0))
                for u in range(8):
                    exps(Step(i, u + 1))
                    copy_turned(Step(i, u))
                    if u in (1, 5):
                        copy_o(Step(i, u - 2))
            att_bodies(act, body)
            copy_o(Step(3, 7))
            for h in range(AH):
                if h >= 4:
                    act.wait_ge(o_summed, h - 3)
                else:
                    act.wait_ge(o_copied, AH)
                act.activation(osq_of(h)[:, :], o_all[:, h, :], ACT.Square).then_inc(o_squared, 1)
            act.wait_ge(o_summed, AH)
            act.activation(orms[:, :, :], pa[:, 0, 0:AH * NC], ACT.Sqrt, bias=eps_col[:, :],
                           scale=1.0 / P).then_inc(o_rms_ready, 1)
            for h in range(AH):
                act.wait_ge(o_normed, h + 1)
                act.activation(o_hi[:, h, :], o_all[:, h, :], ACT.Copy).then_inc(o_hi_ready, 1)

        def att_dve(dve):
            dve.wait_ge(lam_loaded, 16)
            for v in range(2):
                dve.tensor_tensor_reduce(lam_pr[:, v, :], lam_in[:, 2 * v, :], lam_in[:, 2 * v + 1, :],
                                         1.0, 0.0, ALU.mult, ALU.add, lam_s[:, v:v + 1]).then_inc(lam_step, 1)
            dve.wait_ge(lam_exp, 1)
            dve.tensor_tensor(lam[:, :], lam_s[:, 0:1], lam_s[:, 1:2], ALU.subtract).then_inc(lam_step, 1)
            dve.wait_ge(lam_step, 3)
            dve.tensor_scalar(lam[:, :], lam[:, :], LAMBDA_INIT, None, ALU.add).then_inc(lam_step, 1)
            dve.tensor_scalar(g_sub[:, :], gains[:, G["subln"]:G["subln"] + 1], 1.0 - LAMBDA_INIT,
                              None, ALU.mult).then_inc(lam_step, 1)
            dve.wait_ge(lam_step, 5)

            def row_max(s):
                if not s.exists():
                    return
                dve.wait_ge(logits_ready, s.count(1))
                z = pw[:, 2 * s.par:2 * s.par + 2, :]
                dve.memset(z[0:CHUNK, :, s.n - CHUNK:s.n], -1e30).then_inc(masked, 1)
                dve.wait_ge(masked, s.count(1))
                dve.tensor_reduce(mx[s.par][:, :], z[:, :, 0:s.n], AXX, ALU.max).then_inc(max_ready, 1)
                dve.wait_ge(max_ready, s.count(1))
                dve.tensor_scalar(nb[s.par][:, :], mx[s.par][:, :], -SCALE, None, ALU.mult)\
                    .then_inc(bias_ready, 1)

            def combine(s):
                dve.wait_ge(exp_ready, s.count(1) * 2)
                dve.reciprocal(ri[s.par][:, :], rs[s.par][:, :]).then_inc(inv_rows, 1)
                dve.wait_ge(inv_rows, s.count(1))
                dve.tensor_tensor(c1[s.par][:, :], ri[s.par][:, 1:2], lam[:, :], ALU.mult)\
                    .then_inc(lam_rows, 1)
                dve.wait_ge(lam_rows, s.count(1))
                p0, p1 = probs[s.par][:, 0, 0:s.n], probs[s.par][:, 1, 0:s.n]
                dve.tensor_scalar(p1, p1, c1[s.par][:, :], None, ALU.mult).then_inc(second_ready, 1)
                dve.wait_ge(second_ready, s.count(1))
                dve.scalar_tensor_tensor(p0, p0, ri[s.par][:, 0:1], p1, ALU.mult, ALU.subtract)\
                    .then_inc(w_ready, 1)

            def body(i):
                if isinstance(i, int) and i == 0:
                    row_max(Step(0, 0))
                for u in range(8):
                    row_max(Step(i, u + 1))
                    combine(Step(i, u))
            att_bodies(dve, body)
            dve.wait_ge(o_rms_ready, 1)
            dve.reciprocal(oinv[:, :, :], orms[:, :, :]).then_inc(o_inv_ready, 1)

            def normed(h):
                dve.wait_ge(o_spread, h + 1)
                dve.scalar_tensor_tensor(o_all[:, h, :], o_all[:, h, :], g_sub[:, :], pa[:, 2 + h % 2, :],
                                         ALU.mult, ALU.mult).then_inc(o_normed, 1)
            normed(0)
            for h in range(AH):
                if h + 1 < AH:
                    normed(h + 1)
                dve.wait_ge(o_hi_ready, h + 1)
                dve.tensor_tensor(o_lo[:, h, :], o_all[:, h, :], o_hi[:, h, :].bitcast(F32),
                                  ALU.subtract).then_inc(o_split, 1)

        def att_sp(sp):
            sp.wait_ge(heads_ready, 12)
            for r in range(2):
                sp.wait_ge(heads_stored[r], 16 * 7)
            sp.dma_start(lam_in[:, :, :], t["attn_lambda"][0].rearrange("a b -> (a b)")
                         .partition_broadcast(P)).then_inc(lam_loaded, 16)

            def head(i, r):
                h = i * 2 + r
                if not (isinstance(i, int) and i == 0):
                    sp.wait_ge(pv_done, i * 8 + (4 * r - 4))
                for dst, src in ((q_cur[r][:, :], q_dram), (k_cur[r][:, :], k_dram),
                                 (v_cur[r][:, :, :].rearrange("p c e -> p (c e)"), v_dram)):
                    sp.dma_start(dst, src[h] if isinstance(h, int) else
                                 src[bass.ds(h, 1)].rearrange("o p x -> (o p) x"))\
                        .then_inc(head_loaded[r], 16)
            head(0, 0)
            head(0, 1)
            with sp.Fori(1, 4) as i:
                head(i, 0)
                head(i, 1)

        tanh_z = ssm_tanh_z
        cum_ready_v = sem("dt_scaled")

        block = ctx.enter_context(nc.Block())
        ffn_w = {"in0": t["ffn1_w_in"][0], "out0": t["ffn1_w_out"][0],
                 "in1": t["ffn2_w_in"][0], "out1": t["ffn2_w_out"][0],
                 "in2": t["ffn1_w_in"][1], "out2": t["ffn1_w_out"][1],
                 "in3": t["ffn2_w_in"][1], "out3": t["ffn2_w_out"][1]}

        @block.sync
        def _(sp):
            xt = t["x"][0].rearrange("(t p) d -> p t d", p=P)
            for i in range(S // P):
                sp.dma_start(x_in[:, i, :], xt[:, i, :]).then_inc(x_loaded, 16)
            for name in phases:
                if name.startswith("in"):
                    ffn_in_sp(sp, name, ffn_w[name])
                elif name.startswith("out"):
                    out_sp(sp, name, ffn_w[name], KF)
                elif name == "ssm":
                    ssm_sp(sp)
                elif name == "sout":
                    out_sp(sp, name, t["ssm_w_out"][0], KI)
                elif name == "kv":
                    pair_sp(sp, name, t["w_kv"])
                elif name == "q":
                    pair_sp(sp, name, t["attn_w_q"][0])
                elif name == "wo":
                    out_sp(sp, name, t["attn_w_o"][0], AH, between=lambda: att_sp(sp))
            out = t["out"][0].rearrange("(t p) d -> p t d", p=P)
            for i in range(S // P):
                sp.wait_ge(y_copied, 2 * (i + 1))
                sp.dma_start(out[:, i, :], x_out[:, i, :]).then_inc(stored, 16)
            sp.wait_ge(stored, 16 * (S // P))

        @block.gpsimd
        def _(pool):
            pool.memset(ident[:, :], 0.0).then_inc(const_made, 1)
            pool.memset(ones[:, :], 1.0).then_inc(const_made, 1)
            pool.wait_ge(const_made, 2)
            pool.affine_select(out=ident[:, :], in_=ident[:, :], compare_op=ALU.not_equal, fill=1.0,
                               base=0, pattern=[[-1, P]], channel_multiplier=1)\
                .then_inc(const_made, 1)
            pool.memset(buf_b[:, :, :], 0.0).then_inc(sum_cleared, 1)
            pool.wait_ge(sum_cleared, 1)
            with pool.Fori(0, X_PAIRS) as p:
                sum_pool(pool, 0, p)
            pool.affine_select(out=mask[:, :], in_=ones[:, :], compare_op=ALU.is_ge, fill=0.0,
                               base=0, pattern=[[1, P]], channel_multiplier=-1)\
                .then_inc(const_made, 1)
            for name in phases:
                if name == "ssm":
                    ssm_pool(pool)
                if name.startswith("out") or name in ("sout", "wo"):
                    out_pool(pool, name)

        @block.scalar
        def _(act):
            row = 0
            for src, n in ((t["ffn1_norm"], 16), (t["mixer_norm"], 16), (t["ffn2_norm"], 16),
                           (t["kv_norm"], 8), (t["final_norm"], 8), (t["ssm_norm"], 16),
                           (t["ssm_conv_b"], 32), (t["attn_subln"], 1)):
                flat = src.flatten() if len(src.shape) > 1 else src
                act.dma_start(gain_rows[row:row + n, :], flat.rearrange("(r c) -> r c", c=P))\
                    .then_inc(consts_loaded, 16)
                row += n
            act.dma_start(conv_rows[:, :], t["ssm_conv_w"][0].rearrange("k (r c) -> (k r) c", c=P))\
                .then_inc(consts_loaded, 16)
            act.dma_start(dt_bias[DT0:P, :], t["ssm_dt_bias"].rearrange("a h -> h a")).then_inc(ssm_consts, 16)
            act.dma_start(a_neg[DT0:P, :], t["ssm_a_log"].rearrange("a h -> h a")).then_inc(ssm_consts, 16)
            by_half = t["ssm_d"].rearrange("a (j two) -> two (a j)", two=2)
            for half in range(2):
                act.dma_start(dskip[half * 64:(half + 1) * 64, :],
                              by_half[half].partition_broadcast(64), allow_slow_non_contiguous=True).then_inc(ssm_consts, 16)
            for u in range(LEAD):
                hi(act, Units(0, 0, 4), u)
            for p in range(X_PAIRS):
                sq_act(act, 0, p, p)
            for name in phases:
                if name.startswith("in"):
                    ffn_in_act(act, name)
                elif name == "ssm":
                    ssm_act(act)
                elif name == "kv":
                    pair_act(act, name)
                elif name == "q":
                    pair_act(act, name)
                    att_act(act)
                elif name.startswith("out") or name in ("sout", "wo"):
                    out_act(act, name)
            rms_act(act, state_of[last] + 1)

        @block.vector
        def _(dve):
            dve.memset(eps_col[:, :], EPS)
            dve.wait_ge(gains_turned, 1)
            dve.tensor_copy(gains[:, :], pa[:, 0, 0:NG]).then_inc(gains_ready, 1)
            dve.wait_ge(gains_ready, 1)
            dve.wait_ge(conv_turned, 1)
            dve.tensor_scalar(cw[:, 0:4, :], pa[:, 1, 0:P], 0.5, None, ALU.mult).then_inc(cw_ready, 1)
            dve.tensor_scalar(cw[:, 4, :], gains[:, G["conv_b"]:G["conv_b"] + 32], 0.5, None, ALU.mult)\
                .then_inc(cw_ready, 1)
            for p in range(X_PAIRS):
                dve.wait_ge(x_turned, p + 1)
                dve.tensor_copy(x[:, 2 * p:2 * p + 2, :], psum_pair(p)).then_inc(pair_free, 1)
                dve.wait_ge(pair_free, p + 1)
                split_x(dve, 0, p, gain_after("start"), None)
            for u in range(LEAD):
                lo(dve, Units(0, 0, 4), u)
            for name in phases:
                if name.startswith("in"):
                    ffn_in_dve(dve, name)
                elif name.startswith("out"):
                    out_dve(dve, name, 0.5, gain_after(name))
                elif name == "ssm":
                    ssm_dve(dve)
                elif name == "kv":
                    pair_dve(dve, name)
                elif name == "q":
                    pair_dve(dve, name)
                    att_dve(dve)
                elif name in ("sout", "wo"):
                    out_dve(dve, name, 1.0, gain_after(name))
            st = state_of[last] + 1
            rstd_dve(dve, st)
            g = gain_after(last)
            for k in range(KD):
                dve.scalar_tensor_tensor(x[:, k, :], x[:, k, :], gains[:, g + k:g + k + 1], rstd[:, :],
                                         ALU.mult, ALU.mult).then_inc(y_normed, 1)
            for i in range(S // P):
                for half in range(2):
                    n = 2 * i + half
                    dve.wait_ge(y_turned, n + 1)
                    dve.tensor_copy(x_out[:, i, half * S:(half + 1) * S], pa[:, half, :])\
                        .then_inc(y_copied, 1)

        @block.tensor
        def _(pe):
            pe.wait_ge(const_made, 3)
            pe.wait_ge(consts_loaded, 16 * 9)
            pe.transpose(pa[:, 0, 0:NG], gain_rows[:, :], ident[0:NG, 0:NG]).then_inc(gains_turned, 1)
            pe.transpose(pa[:, 1, 0:P], conv_rows[:, :], ident[:, :]).then_inc(conv_turned, 1)
            pe.wait_ge(x_loaded, 16 * (S // P))
            for p in range(X_PAIRS):
                if p >= 2:
                    pe.wait_ge(pair_free, p - 1)
                for o in range(2):
                    for i in range(S // P):
                        last_t = pe.transpose(psum_pair(p)[:, o, i * P:(i + 1) * P],
                                              x_in[:, i, (2 * p + o) * P:(2 * p + o + 1) * P],
                                              ident[:, :])
                last_t.then_inc(x_turned, 1)
            for name in phases:
                if name.startswith("in"):
                    ffn_in_pe(pe, name)
                elif name.startswith("out"):
                    out_pe(pe, name, KF, hh, hl, ffn_out_ready(pe, name))
                elif name == "ssm":
                    ssm_pe(pe)
                elif name == "sout":
                    out_pe(pe, name, KI, y_hi, y_lo, lambda u: pe.wait_ge(y_split, u + 1))
                elif name == "kv":
                    pair_pe(pe, name)
                elif name == "q":
                    pair_pe(pe, name)
                    att_pe(pe)
                elif name == "wo":
                    out_pe(pe, name, AH, o_hi, o_lo, lambda u: pe.wait_ge(o_split, 4 * u + 4))
            stats(pe, state_of[last] + 1)
            spread_stats(pe, state_of[last] + 1)
            for i in range(S // P):
                for half in range(2):
                    n = 2 * i + half
                    if n >= 2:
                        pe.wait_ge(y_copied, n - 1)
                    for k in range(4 * half, 4 * half + 4):
                        if i == 0:
                            pe.wait_ge(y_normed, k + 1)
                        l = pe.transpose(pa[:, half, (k % 4) * P:(k % 4 + 1) * P],
                                         x[:, k, i * P:(i + 1) * P], ident[:, :])
                    l.then_inc(y_turned, 1)


_INS = ["x", "ffn1_norm", "ffn1_w_in", "ffn1_w_out", "mixer_norm", "ffn2_norm", "ffn2_w_in",
        "ffn2_w_out", "ssm_w_in", "ssm_conv_w", "ssm_conv_b", "ssm_dt_bias", "ssm_a_log", "ssm_d",
        "ssm_norm", "ssm_w_out", "kv_norm", "w_kv", "attn_w_q", "attn_lambda", "attn_subln",
        "attn_w_o", "final_norm"]


def tables():
    half = 32
    inv = np.float32(10000.0) ** (-np.arange(0, 2 * half, 2, dtype=np.float32) / np.float32(2 * half))
    ang = np.arange(S, dtype=np.float32)[None, :] * inv[:, None].astype(np.float32)
    rows = np.arange(P) % half
    rope = np.stack([np.cos(ang)[rows], np.sin(ang)[rows]]).astype(np.float32)
    swap = np.zeros((P, P), np.float32)
    for m in range(P):
        if m % (2 * half) < half:
            swap[m + half, m] = -1.0
        else:
            swap[m - half, m] = 1.0
    return {"rope_tables": rope, "rope_rotation": swap}


def kernel(**inputs):
    import concourse.bacc as bacc
    from concourse.bass_utils import run_bass_kernel_spmd

    nc = bacc.Bacc("TRN2", target_bir_lowering=False, num_devices=1)
    arrays, t = {}, {}
    for name, a in {**{n: inputs[n] for n in _INS}, **tables()}.items():
        a = np.ascontiguousarray(a)
        arrays[f"in_{name}"] = a
        t[name] = nc.dram_tensor(f"in_{name}", a.shape, mybir.dt.from_np(a.dtype),
                                 kind="ExternalInput").ap()
    t["out"] = nc.dram_tensor("out_y", (1, S, D), F32, kind="ExternalOutput").ap()
    build_trunk(nc, t)
    r = run_bass_kernel_spmd(nc, [arrays], core_ids=[0])
    return r.results[0]["out_y"]
```

```python
from contextlib import ExitStack
import math

import numpy as np
import concourse.bass as bass
from concourse import mybir

F32 = mybir.dt.float32
F32R = mybir.dt.float32r
ALU = mybir.AluOpType
ACT = mybir.ActivationFunctionType
AXX = mybir.AxisListType.X

P = 128
S = 512
D = 1024
KD = D // P
F = 2816
KF = F // P
DI = 2048
GROUPS = 8
HG = 4
HEADS = 32
HP = 64
NST = 128
KI = DI // P
L = 128
NC = S // L
EPS = 1e-5
AH = 8
CHUNK = 64
LAMBDA_INIT = 0.8 - 0.6 * math.exp(-0.3)
SCALE = 64 ** -0.5

SLOTS = 4
UK = 4
LEAD = 3

PHASES = [("in0", 22, 2), ("out0", 4, 6), ("ssm", 24, 2), ("sout", 4, 4), ("in1", 22, 2),
          ("out1", 4, 6), ("kv", 8, 2), ("in2", 22, 2), ("out2", 4, 6), ("q", 4, 2), ("wo", 4, 2),
          ("in3", 22, 2), ("out3", 4, 6)]
X_PAIRS = KD // 2


def plan(stop):
    unit, pair, at = 0, X_PAIRS, {}
    phases = []
    for name, pairs, units in PHASES:
        assert unit % SLOTS == 0 and pair % 2 == 0
        at[name] = (unit, pair, pairs, units)
        phases.append(name)
        unit += pairs * units
        pair += pairs
        if name == stop:
            break
    return at, phases, unit


def build_trunk(nc, t, stop=None):
    at, phases, n_units = plan(stop)
    last = phases[-1]
    ctx = ExitStack()
    with ctx:
        base = (nc.sbuf_base + 63) // 32 * 32
        end = nc.sbuf_top

        class Region:

            def __init__(self, start, size):
                self.at, self.end = start, start + size

            def tile(self, name, shape, dtype=F32):
                size = 4 * math.prod(shape[1:])
                size = (size + 31) // 32 * 32
                assert self.at + size <= self.end, (name, self.at + size - self.end)
                got = nc.alloc_sbuf_tensor_at(name, shape, dtype, offset=self.at)
                self.at += size
                return got

        glob = Region(base, end - base)
        arena_size = 2 * KF * S * 4
        x = glob.tile("x_t", [P, KD, S])
        xh_off = glob.at
        xh = glob.tile("x_hi", [P, KD, S], F32R)
        xl = glob.tile("x_lo", [P, KD, S], F32R)
        x_gain = Region(xh_off, KD * S * 4).tile("x_times_gain", [P, KD, S])
        x_out = Region(xh_off + KD * S * 4, S // P * D * 4).tile("x_out", [P, S // P, D])
        raw = [glob.tile(f"w_raw{s}", [P, UK * 256]) for s in range(SLOTS)]
        whi = [glob.tile(f"w_hi{s}", [P, UK * 256], F32R) for s in range(SLOTS)]
        wlo = [glob.tile(f"w_lo{s}", [P, UK * 256], F32R) for s in range(SLOTS)]
        rstd = glob.tile("rstd", [P, S])
        rms_tok = glob.tile("rms_tok", [P, S // P])
        inv_tok = glob.tile("inv_rms_tok", [P, S // P])
        buf_a = glob.tile("gate_or_squares", [P, 2, S])
        buf_b = glob.tile("up_or_square_sum", [P, 2, S])
        ident = glob.tile("ident", [P, P])
        ones = glob.tile("ones", [P, P])
        NG = 16 + 16 + 16 + 8 + 8 + 16 + 32 + 1
        gains = glob.tile("gains", [P, NG])
        arena_off = glob.at
        assert arena_off + arena_size <= end, (arena_off, arena_size, end)
        rest = Region(arena_off + arena_size, end - arena_off - arena_size)

        ffn = Region(arena_off, arena_size)
        hh = ffn.tile("hidden_hi", [P, KF, S], F32R)
        hl = ffn.tile("hidden_lo", [P, KF, S], F32R)
        first = Region(arena_off, arena_size)
        x_in = first.tile("x_in", [P, S // P, D])
        first_rows = first.tile("first_gain_rows", [16, P])
        gain_rows = rest.tile("gain_rows", [NG - 16, P])

        conv_rows = rest.tile("conv_rows", [P, P])

        ssm = Region(arena_off, arena_size)
        y32 = ssm.tile("y_t", [P, KI, S])
        group_off = ssm.at
        PRE = S + 4

        def scan_buffers(region, tag):
            return (region.tile("decay_or_m" + tag, [P, HG, S]), region.tile("cum_or_c" + tag, [P, HG, S]),
                    region.tile("x_dt" + tag, [P, NC, HG * HP]),
                    region.tile("x_dt_to_end" + tag, [P, NC, HG * HP]),
                    region.tile("b_tok" + tag, [P, NC, NST]))
        scan_main = scan_buffers(ssm, "")
        scan_size = ssm.at - group_off
        scan_last = scan_buffers(Region(xh_off, 2 * KD * S * 4), "_last")
        pre_x = ssm.tile("conv_in_x", [P, 2, PRE])
        xv = [ssm.tile(f"conv_out_x{r}", [P, 2, S]) for r in range(2)]
        pre_bc = ssm.tile("conv_in_bc", [P, 2, PRE])
        bcv = ssm.tile("conv_out_bc", [P, 2, S])
        tanh = ssm.tile("tanh", [P, 4, S])
        cbm = rest.tile("cb_masked", [P, S])
        prev = rest.tile("state_before", [P, NC - 1, HG * HP])
        cw = rest.tile("conv_w_b", [P, 5, 32])
        dskip = rest.tile("d_skip", [P, KI])
        mask = rest.tile("causal", [P, P])
        tok_all = rest.tile("cum_dt_tok", [P, 2, NC, HEADS])
        gtok = rest.tile("cum_dt_group", [P, 2, NC, HG])
        dte = rest.tile("to_end", [P, NC, HG])
        cd = rest.tile("block_decay", [P, HG, NC])
        gcw = [rest.tile(f"group_conv{r}", [P, 5, 4]) for r in range(2)]
        gdn = [rest.tile(f"group_d_norm{r}", [P, 2, 2]) for r in range(2)]
        dt_bias = rest.tile("dt_bias", [P, 1])
        a_neg = rest.tile("minus_a", [P, 1])
        yrms = rest.tile("y_rms", [P, NC])
        yinv = rest.tile("y_inv_rms", [P, NC])
        DT0 = P - HEADS
        dtr = Region(group_off, scan_size)
        wdt = dtr.tile("w_dt", [P, KD, P])
        wdt_hi = dtr.tile("w_dt_hi", [P, KD, P], F32R)
        wdt_lo = dtr.tile("w_dt_lo", [P, KD, P], F32R)
        dt_raw = dtr.tile("dt_raw", [P, S])
        dt_e = dtr.tile("dt_e", [P, S])
        dt_u = dtr.tile("dt_u", [P, S])
        dt_ln = dtr.tile("dt_ln", [P, S])
        dt_r = dtr.tile("dt_r", [P, S])
        dt_t = dtr.tile("dt_t", [P, S])
        dt_c = dtr.tile("dt_c", [P, S])
        y_hi = Region(group_off, KI * S * 4).tile("y_hi", [P, KI, S], F32R)
        y_lo = Region(arena_off, KI * S * 4).tile("y_lo", [P, KI, S], F32R)
        rope = Region(arena_off, arena_size)
        cos_t = rope.tile("cos_t", [P, S])
        sin_t = rope.tile("sin_t", [P, S])
        rot = rope.tile("rot", [P, P])
        heads_out = [rope.tile(f"heads_out{r}", [P, 2, S]) for r in range(2)]
        att = Region(rope.at, arena_off + arena_size - rope.at)
        o_all = att.tile("o_t", [P, AH, S])
        o_hi = att.tile("o_hi", [P, AH, S], F32R)
        o_lo = att.tile("o_lo", [P, AH, S], F32R)
        q_cur = [att.tile(f"q_cur{r}", [P, S]) for r in range(2)]
        k_cur = [att.tile(f"k_cur{r}", [P, S]) for r in range(2)]
        v_cur = [att.tile(f"v_cur{r}", [P, NC, P]) for r in range(2)]
        probs = [att.tile(f"probs{r}", [P, 2, S]) for r in range(2)]
        w_t = [att.tile(f"w_t{r}", [P, S]) for r in range(2)]
        lam_in = att.tile("lam_in", [P, 4, HP])
        lam_pr = att.tile("lam_products", [P, 2, HP])
        lam_s = rest.tile("lam_sums", [P, 2])
        lam = rest.tile("lam", [P, 1])
        nb = [rest.tile(f"minus_max{r}", [P, 2]) for r in range(2)]
        rs = [rest.tile(f"row_sum{r}", [P, 2]) for r in range(2)]
        ri = [rest.tile(f"row_inv{r}", [P, 2]) for r in range(2)]
        c1 = [rest.tile(f"lam_inv{r}", [P, 1]) for r in range(2)]
        orms = rest.tile("o_rms", [P, AH, NC])
        oinv = rest.tile("o_inv_rms", [P, AH, NC])
        g_sub = rest.tile("subln_gain", [P, 1])
        q_dram = nc.dram_tensor("q_scratch", [AH, P, S], F32, kind="Internal").ap()
        k_dram = nc.dram_tensor("k_scratch", [AH, P, S], F32, kind="Internal").ap()
        v_dram = nc.dram_tensor("v_scratch", [AH, P, S], F32, kind="Internal").ap()
        cum_dram = nc.dram_tensor("cum_scratch", [HEADS, S], F32, kind="Internal").ap()

        G = {}
        col = 0
        for name, n in (("ffn1", 16), ("mixer", 16), ("ffn2", 16), ("kv", 8), ("final", 8),
                        ("ssm_norm", 16), ("conv_b", 32), ("subln", 1)):
            G[name] = col
            col += n

        pw = ctx.enter_context(nc.psum_tensor("psum_pairs", [P, 4, S], F32))
        pa = ctx.enter_context(nc.psum_tensor("psum_other", [P, 4, S], F32))

        def sem(name):
            return ctx.enter_context(nc.semaphore(name))

        unit_loaded = [sem(f"unit_loaded{s}") for s in range(SLOTS)]
        hi_ready = sem("hi_ready")
        lo_ready = sem("lo_ready")
        unit_used = sem("unit_used")
        pair_free = sem("pair_free")
        first_gains_loaded = sem("first_gains_loaded")
        consts_loaded = sem("consts_loaded")
        x_loaded = [sem(f"x_loaded{p}") for p in range(X_PAIRS)]
        const_made = sem("const_made")
        first_gains_turned = sem("first_gains_turned")
        first_gains_ready = sem("first_gains_ready")
        gains_turned = sem("gains_turned")
        gains_ready = sem("gains_ready")
        x_turned = sem("x_turned")
        x_hi_ready = sem("x_hi_ready")
        x_split = sem("x_split")
        squared = sem("squared")
        sum_cleared = sem("sum_cleared")
        summed = sem("summed")
        halved = sem("halved")
        part_added = sem("part_added")
        early_sums = sem("early_sums")
        last_squares = sem("last_squares")
        stat_ready = sem("stat_ready")
        rms_ready = sem("rms_ready")
        inv_ready = sem("inv_ready")
        spread_ready = sem("spread_ready")
        rstd_ready = sem("rstd_ready")
        silu_done = sem("silu_done")
        hid_made = sem("hid_made")
        hid_hi = sem("hid_hi")
        hid_ready = sem("hid_ready")
        x_scaled = sem("x_scaled")
        y_turned = sem("y_turned")
        out_copied = sem("out_copied")
        left_ready = sem("left_ready")
        right_ready = sem("right_ready")
        stored = sem("stored")
        rope_loaded = sem("rope_loaded")
        head_rotated = sem("head_rotated")
        rope_cos = sem("rope_cos")
        rope_sin = sem("rope_sin")
        heads_ready = sem("heads_ready")
        heads_stored = [sem(f"heads_stored{r}") for r in range(2)]
        lam_loaded = sem("lam_loaded")
        lam_step = sem("lam_step")
        lam_exp = sem("lam_exp")
        head_loaded = [sem(f"head_loaded{r}") for r in range(2)]
        logits_ready = sem("logits_ready")
        masked = sem("masked")
        bias_ready = sem("bias_ready")
        exp_ready = sem("exp_ready")
        inv_rows = sem("inv_rows")
        lam_rows = sem("lam_rows")
        second_ready = sem("second_ready")
        w_ready = sem("w_ready")
        w_turned = sem("w_turned")
        wt_ready = sem("wt_ready")
        pv_done = sem("pv_done")
        o_copied = sem("o_copied")
        o_squared = sem("o_squared")
        o_summed = sem("o_summed")
        o_rms_ready = sem("o_rms_ready")
        o_inv_ready = sem("o_inv_ready")
        o_spread = sem("o_spread")
        o_normed = sem("o_normed")
        o_hi_ready = sem("o_hi_ready")
        o_split = sem("o_split")
        ssm_consts = sem("ssm_consts")
        conv_turned = sem("conv_turned")
        cw_ready = sem("cw_ready")
        wdt_loaded = sem("wdt_loaded")
        wdt_hi_ready = sem("wdt_hi_ready")
        wdt_ready = sem("wdt_ready")
        dt_used = sem("dt_product")
        dt_v = sem("dt_vector_step")
        dt_s = sem("dt_scalar_step")
        cum_stored = sem("cum_stored")
        cum_ready = sem("cum_ready")
        tok_turned = sem("tok_turned")
        tok_ready = sem("tok_ready")
        halo_ready = sem("halo_ready")
        params_ready = sem("params_ready")
        cum_loaded = sem("cum_loaded")
        conv_base_x = sem("conv_base_x")
        conv_base_bc = sem("conv_base_bc")
        conv_tap_x = sem("conv_tap_x")
        conv_tap_bc = sem("conv_tap_bc")
        conv_tanh_x = sem("conv_tanh_x")
        conv_tanh_bc = sem("conv_tanh_bc")
        conv_done = sem("conv_done")
        z_tanh = sem("z_tanh")
        z_ready = sem("z_ready")
        z_product = sem("z_product")
        gtok_ready = sem("gtok_ready")
        dte_diff = sem("dte_diff")
        dte_ready = sem("dte_ready")
        seg_ready = sem("seg_ready")
        decay_ready = sem("decay_ready")
        growth_ready = sem("growth_ready")
        cd_ready = sem("cd_ready")
        turned_a = sem("x_b_turned")
        cb_product = sem("cb_product")
        btok_ready = sem("btok_ready")
        xdt_ready = sem("xdt_ready")
        cbm_ready = sem("cbm_ready")
        xde_ready = sem("xde_ready")
        m_ready = sem("m_ready")
        c_ready = sem("c_ready")
        states_product = sem("states_product")
        prev_step = sem("prev_step")
        y_product = sem("y_product")
        y_plus = sem("y_plus_skip")
        y_gated = sem("y_gated")
        y_squared = sem("y_squared")
        y_halved = sem("y_halved")
        y_stat = sem("y_stat")
        y_rms = sem("y_rms_ready")
        y_inv = sem("y_inv_ready")
        y_spread = sem("y_spread")
        y_final = sem("y_final")
        yhi_ready = sem("yhi_ready")
        y_split = sem("y_split")

        def psum_pair(j):
            return pw[:, 2 * (j % 2):2 * (j % 2) + 2, :]

        def bc(ap, n):
            return ap.unsqueeze(1).broadcast_to((ap.shape[0], n, ap.shape[1]))

        FFN_STEPS = 11
        ffn_base, norm_no, n = {}, {}, 0
        for name in phases:
            if name.startswith("in"):
                ffn_base[name] = n
                n += FFN_STEPS
        state = 0
        splits_before = {}
        splits = X_PAIRS
        state_of = {}
        for name in phases:
            if name == "in2":
                splits += X_PAIRS
            state_of[name] = state
            splits_before[name] = splits
            if name.startswith("out") or name in ("sout", "wo"):
                state += 1
                splits += X_PAIRS

        final_state = state_of[last] + 1

        def gain_after(name):
            return {"start": G["ffn1"], "out0": G["mixer"], "sout": G["ffn2"], "out1": G["kv"],
                    "kv": G["ffn1"] + 8, "out2": G["mixer"] + 8, "wo": G["ffn2"] + 8,
                    "out3": G["final"]}[name]


        class Units:

            def __init__(self, n0, body, per):
                self.n0, self.body, self.per = n0, body, per

            def slot(self, u):
                return (self.n0 + u) % SLOTS

            def number(self, u):
                return self.body * self.per + (self.n0 + u)

            def loads(self, u):
                return self.body * (16 * self.per // SLOTS) + 16 * ((self.n0 + u) // SLOTS + 1)

        def hi(act, units, u):
            if isinstance(units.body, int) and units.number(u) >= n_units:
                return
            j = units.slot(u)
            act.wait_ge(unit_loaded[j], units.loads(u))
            if not (isinstance(units.body, int) and units.number(u) < SLOTS):
                act.wait_ge(unit_used, units.number(u) - SLOTS + 1)
            act.activation(whi[j][:, :], raw[j][:, :], ACT.Copy).then_inc(hi_ready, 1)

        def lo(dve, units, u):
            if isinstance(units.body, int) and units.number(u) >= n_units:
                return
            j = units.slot(u)
            dve.wait_ge(hi_ready, units.number(u) + 1)
            dve.tensor_tensor(wlo[j][:, :], raw[j][:, :], whi[j][:, :].bitcast(F32),
                              ALU.subtract).then_inc(lo_ready, 1)

        def products(pe, units, u, out, views, last_of_pair, x_hi, x_lo, wait=True):
            j = units.slot(u)
            pe.wait_ge(lo_ready, units.number(u) + 1)
            for o, ks in views:
                for c, (k, first, w0, last_k) in enumerate(ks):
                    wh, wl = whi[j][:, w0:w0 + P], wlo[j][:, w0:w0 + P]
                    pe.matmul(out[:, o, :], wh, x_hi[:, k, :], start=first, stop=False)
                    pe.matmul(out[:, o, :], wh, x_lo[:, k, :], start=False, stop=False)
                    last = pe.matmul(out[:, o, :], wl, x_hi[:, k, :], start=False, stop=last_k)
            last.then_inc(unit_used, 1)

        def k_views(k0, nk, n_k):
            return [(o, [(k0 + kk, k0 + kk == 0, kk * 256 + o * P, k0 + kk == n_k - 1)
                         for kk in range(nk)]) for o in range(2)]

        def row_unit(w, k0, nk, c0):
            return w.rearrange("(k p) c -> p k c", p=P)[:, k0:k0 + nk, bass.ds(c0, 256)]

        def in_pairs(pe, name, i, q0, n0, stat=False):
            units = Units(n0, i, 4)
            for r in range(2):
                start = name == "in0" and isinstance(i, int)
                if start and r:
                    pe.wait_ge(pair_free, X_PAIRS)
                if not start:
                    pe.wait_ge(pair_free, i * 2 + (q0 + r - 1))
                for u in range(2):
                    if stat and r == 0:
                        pe.wait_ge(x_split, splits_before[name] - X_PAIRS + 2 * u + 2)
                    products(pe, units, 2 * r + u, psum_pair(r), k_views(4 * u, 4, KD), u == 1,
                             xh, xl)
                    if stat and name == "in2" and (r, u) == (0, 0):
                        rotate(pe, PairSlot("kv", 0, at["kv"][2]))
                    if start:
                        if (r, u) == (1, 0):
                            stats(pe, 0)
                        elif (r, u) == (1, 1):
                            spread_stats(pe, 0)
                    elif stat and r == 0 and name != "in2":
                        (stats, spread_stats)[u](pe, state_of[name])

        def stats(pe, state):
            pe.wait_ge(const_made, 3)
            pe.wait_ge(summed, X_PAIRS * (state + 1))
            token_sums(pe, buf_b[:, 0, :], stat_ready)

        def token_sums(pe, squares, done):
            for c in range(S // P):
                l = pe.matmul(pa[:, 3, c:c + 1], squares[:, c * P:(c + 1) * P], ones[:, 0:1],
                              start=True, stop=True)
            l.then_inc(done, 1)

        def spread_rows(pe, column, done):
            for c in range(S // P):
                last = pe.matmul(pa[:, 3, c * P:(c + 1) * P],
                                 column[:, c:c + 1].broadcast_to((P, P)), ident[:, :],
                                 start=True, stop=True)
            last.then_inc(done, 1)

        def spread_stats(pe, state):
            pe.wait_ge(inv_ready, state + 1)
            spread_rows(pe, inv_tok, spread_ready)

        def rms_act(act, state):
            act.wait_ge(stat_ready, state + 1)
            act.activation(rms_tok[:, :], pa[:, 3, 0:S // P], ACT.Sqrt, bias=eps_col[:, :],
                           scale=1.0 / D).then_inc(rms_ready, 1)

        def rstd_dve(dve, state):
            dve.wait_ge(rms_ready, state + 1)
            dve.reciprocal(inv_tok[:, :], rms_tok[:, :]).then_inc(inv_ready, 1)
            dve.wait_ge(spread_ready, state + 1)
            dve.tensor_copy(rstd[:, :], pa[:, 3, :]).then_inc(rstd_ready, 1)
            dve.wait_ge(rstd_ready, state + 1)

        def split_x(dve, m, p, gain):
            for o in range(2):
                k = 2 * p + o
                g = gains[:, gain + k:gain + k + 1] if isinstance(k, int) else \
                    gains[:, bass.ds(k + gain, 1)]
                xs = x[:, k, :] if isinstance(k, int) else x[:, bass.ds(k, 1), :].squeeze(1)
                h = xh[:, k, :] if isinstance(k, int) else xh[:, bass.ds(k, 1), :].squeeze(1)
                l = xl[:, k, :] if isinstance(k, int) else xl[:, bass.ds(k, 1), :].squeeze(1)
                dve.tensor_scalar(h, xs, g, None, ALU.mult).then_inc(x_hi_ready, 1)
                dve.wait_ge(x_hi_ready, (m + p) * 2 + (o + 1))
                ins = dve.scalar_tensor_tensor(l, xs, g, h.bitcast(F32), ALU.mult, ALU.subtract)
            ins.then_inc(x_split, 1)

        def sq_act(act, state, p, q):
            act.wait_ge(pair_free, q + 1)
            act.wait_ge(summed, state * X_PAIRS + p)
            xs = x[:, 2 * p:2 * p + 2, :] if isinstance(p, int) else x[:, bass.ds(p * 2, 2), :]
            act.activation(buf_a[:, :, :], xs, ACT.Square).then_inc(squared, 1)

        def halve(pool, state):
            pool.wait_ge(summed, state * X_PAIRS + X_PAIRS - 1)
            pool.tensor_tensor(buf_b[:, 0, :], buf_b[:, 0, :], buf_b[:, 1, :], ALU.add)\
                .then_inc(halved, 1)
            if state == final_state:
                return
            pool.wait_ge(halved, state + 1)
            pool.wait_ge(squared, state * X_PAIRS + X_PAIRS - 1)
            for o in range(2):
                if o:
                    pool.wait_ge(part_added, state + 1)
                pool.tensor_tensor(buf_b[:, 0, :], buf_b[:, 0, :], buf_a[:, o, :], ALU.add)\
                    .then_inc((part_added, summed)[o], 1)

        def sum_pool(pool, state, p):
            pool.wait_ge(squared, p + state * X_PAIRS)
            pool.tensor_tensor(buf_b[:, :, :], buf_b[:, :, :], buf_a[:, :, :],
                               ALU.add).then_inc(summed, 1)

        def residual(dve, name, i, r, used, scale, gain):
            p = i * 2 + r
            dve.wait_ge(unit_used, used)
            xs = x[:, 2 * p:2 * p + 2, :] if isinstance(p, int) else x[:, bass.ds(p * 2, 2), :]
            dve.scalar_tensor_tensor(xs, psum_pair(r), scale, xs, ALU.mult, ALU.add)\
                .then_inc(pair_free, 1)
            dve.wait_ge(pair_free, p + (at[name][1] + 1))
            if name == last:
                for k in (2 * p, 2 * p + 1):
                    ins = dve.tensor_scalar(x_gain[:, k, :], x[:, k, :], gains[:, gain + k:gain + k + 1],
                                            None, ALU.mult)
                ins.then_inc(x_scaled, 1)
                return
            split_x(dve, splits_before[name], p, gain)

        def out_dve(dve, name, scale, gain):
            n0, q0, pairs, per = at[name]

            def body(i):
                units = Units(n0, i, 2 * per)
                for r in range(2):
                    for u in range(per):
                        lo(dve, units, r * per + u + LEAD)
                    residual(dve, name, i, r, units.number((r + 1) * per), scale, gain)
            if name == "sout":
                body(1)
            elif name == last:
                for i in range(2):
                    body(i)
            else:
                with dve.Fori(0, 2) as i:
                    body(i)

        def out_act(act, name):
            n0, q0, pairs, per = at[name]

            def body(i):
                units = Units(n0, i, 2 * per)
                for r in range(2):
                    for u in range(per):
                        hi(act, units, r * per + u + LEAD)
                        if name == last and i * 2 + r and u == 2:
                            out_copy(act, i * 2 + r - 1)
                    sq_act(act, state_of[name] + 1, i * 2 + r, i * 2 + (q0 + r))
            if name == "sout":
                body(1)
            elif name == last:
                for i in range(2):
                    body(i)
            else:
                with act.Fori(0, 2) as i:
                    body(i)

        def out_pool(pool, name):
            state = state_of[name] + 1
            done = [v + FFN_STEPS for k, v in ffn_base.items() if phases.index(k) < phases.index(name)]
            if name == "sout":
                pool.wait_ge(y_final, GROUPS)
            if name == "wo":
                pool.wait_ge(o_summed, AH)
            pool.wait_ge(hid_ready, max(done))
            pool.memset(buf_b[:, :, :], 0.0).then_inc(sum_cleared, 1)
            pool.wait_ge(sum_cleared, state)
            with pool.Fori(0, X_PAIRS - 1) as p:
                sum_pool(pool, state, p)
            halve(pool, state)

        SOUT_ORDER = ((0, 0), (0, 1), (1, 0), (1, 1), (0, 2), (1, 2), (0, 3), (1, 3))

        def out_pe(pe, name, n_k, v_hi, v_lo, ready):
            n0, q0, pairs, per = at[name]

            def body(i):
                units = Units(n0, i, 2 * per)
                for r in range(2):
                    pe.wait_ge(pair_free, i * 2 + (q0 + r - 1))
                    for u in range(per):
                        if r == 0:
                            ready(u)
                        products(pe, units, r * per + u, psum_pair(r),
                                 k_views(UK * u, min(UK, n_k - UK * u), n_k), u == per - 1, v_hi, v_lo)
                        if name == last and i * 2 + r and u == 1:
                            turn_out(pe, i * 2 + r - 1)
                        if name == last and (i, r, u) == (1, 1, 3):
                            pe.wait_ge(halved, final_state + 1)
                            last_sums(pe, buf_b[:, 0, :], True)
            if name == last:
                for i in range(2):
                    body(i)
                turn_out(pe, X_PAIRS - 1)
                pe.wait_ge(last_squares, 1)
                last_sums(pe, buf_a[:, 0, :], False)
                return
            with pe.Fori(1 if name == "sout" else 0, 2) as i:
                body(i)

        def last_sums(pe, squares, first_part):
            for c in range(S // P):
                l = pe.matmul(pa[:, 3, c:c + 1], squares[:, c * P:(c + 1) * P], ones[:, 0:1],
                              start=first_part and c == 0, stop=not first_part and c == S // P - 1)
            l.then_inc(early_sums if first_part else stat_ready, 1)

        def turn_out(pe, p):
            pe.wait_ge(x_scaled, p + 1)
            if p:
                pe.wait_ge(out_copied, p)
            for i in range(S // P):
                for o in range(2):
                    c = (i % 2) * 256 + o * P
                    l = pe.transpose(pa[:, i // 2, c:c + P], x_gain[:, 2 * p + o, i * P:(i + 1) * P],
                                     ident[:, :])
            l.then_inc(y_turned, 1)

        def out_block(p):
            return pa[:, 0:2, :].rearrange("p b (h c) -> p (b h) c", h=2)

        def out_copy(act, p):
            act.wait_ge(y_turned, p + 1)
            act.activation(x_out[:, :, p * 256:(p + 1) * 256], out_block(p), ACT.Copy)\
                .then_inc(out_copied, 1)

        def out_sp(sp, name, w, n_k, between=None):
            n0, q0, pairs, per = at[name]

            def body(i):
                units = Units(n0, i, 2 * per)
                for r in range(2):
                    for u in range(per):
                        nk = min(UK, n_k - UK * u)
                        load(sp, units, r * per + u, row_unit(w, UK * u, nk, i * 512 + r * 256), nk)
            if name == "sout":
                units = Units(n0, 0, 2 * per)
                for n, (r, u) in enumerate(SOUT_ORDER):
                    load(sp, units, n, row_unit(w, UK * u, UK, r * 256))
                body(1)
                return
            if between is not None:
                body(0)
                between()
                body(1)
                return
            with sp.Fori(0, 2) as i:
                body(i)

        def load(sp, units, u, source, nk=UK, wide=256):
            j = units.slot(u)
            if not (isinstance(units.body, int) and units.number(u) < SLOTS):
                sp.wait_ge(lo_ready, units.number(u) - SLOTS + 1)
            dest = raw[j][:, 0:nk * 256].rearrange("p (k c) -> p k c", c=wide)
            sp.dma_start(dest, source).then_inc(unit_loaded[j], 16)

        def load_x(sp, p):
            d = slice(p * 256, (p + 1) * 256)
            sp.dma_start(x_in[:, :, d], t["x"][0].rearrange("(t p) d -> p t d", p=P)[:, :, d])\
                .then_inc(x_loaded[p], 16)

        def turned_banks(p):
            return pw[:, 2:4, :] if p % 2 else pa[:, 0:2, :]

        def turn_x(pe, p):
            pe.wait_ge(x_loaded[p], 16)
            if p >= 2:
                pe.wait_ge(pair_free, p - 1)
            for o in range(2):
                for i in range(S // P):
                    last_t = pe.transpose(turned_banks(p)[:, o, i * P:(i + 1) * P],
                                          x_in[:, i, (2 * p + o) * P:(2 * p + o + 1) * P], ident[:, :])
            last_t.then_inc(x_turned, 1)

        def load_consts(act):
            row = 0
            for src, n in ((t["mixer_norm"], 16), (t["ffn2_norm"], 16), (t["kv_norm"], 8),
                           (t["final_norm"], 8), (t["ssm_norm"], 16), (t["ssm_conv_b"], 32),
                           (t["attn_subln"], 1)):
                flat = src.flatten() if len(src.shape) > 1 else src
                act.dma_start(gain_rows[row:row + n, :], flat.rearrange("(r c) -> r c", c=P))\
                    .then_inc(consts_loaded, 16)
                row += n
            act.dma_start(conv_rows[:, :], t["ssm_conv_w"][0].rearrange("k (r c) -> (k r) c", c=P))\
                .then_inc(consts_loaded, 16)
            act.dma_start(dt_bias[DT0:P, :], t["ssm_dt_bias"].rearrange("a h -> h a"))\
                .then_inc(ssm_consts, 16)
            act.dma_start(a_neg[DT0:P, :], t["ssm_a_log"].rearrange("a h -> h a")).then_inc(ssm_consts, 16)
            by_half = t["ssm_d"].rearrange("a (j two) -> two (a j)", two=2)
            for half in range(2):
                act.dma_start(dskip[half * 64:(half + 1) * 64, :],
                              by_half[half].partition_broadcast(64), allow_slow_non_contiguous=True)\
                    .then_inc(ssm_consts, 16)

        def keep_consts(dve):
            dve.wait_ge(gains_turned, 1)
            dve.tensor_copy(gains[:, 16:NG], pa[:, 0, 0:NG - 16]).then_inc(gains_ready, 1)
            dve.wait_ge(gains_ready, 1)
            dve.wait_ge(conv_turned, 1)
            dve.tensor_scalar(cw[:, 0:4, :], pa[:, 1, 0:P], 0.5, None, ALU.mult).then_inc(cw_ready, 1)
            dve.tensor_scalar(cw[:, 4, :], gains[:, G["conv_b"]:G["conv_b"] + 32], 0.5, None, ALU.mult)\
                .then_inc(cw_ready, 1)

        def ffn_in_sp(sp, name, w):
            n0, q0, pairs, per = at[name]

            def body(i):
                units = Units(n0, i, 4)
                for r in range(2):
                    for u in range(2):
                        load(sp, units, 2 * r + u, row_unit(w, UK * u, UK, i * 256 + r * F))
                        if name == "in0" and isinstance(i, int) and r == 0:
                            load_x(sp, 2 + u)
            ffn_steps(sp, n0, body)

        def ffn_in_pe(pe, name):
            n0, q0, pairs, per = at[name]
            in_pairs(pe, name, 0, q0, n0, stat=True)
            with pe.Fori(1, FFN_STEPS) as i:
                in_pairs(pe, name, i, q0, n0)
            if name == "in0":
                pe.wait_ge(consts_loaded, 16 * 8)
                pe.transpose(pa[:, 0, 0:NG - 16], gain_rows[:, :], ident[0:NG - 16, 0:NG - 16])\
                    .then_inc(gains_turned, 1)
                pe.transpose(pa[:, 1, 0:P], conv_rows[:, :], ident[:, :]).then_inc(conv_turned, 1)

        def ffn_in_act(act, name):
            n0, q0, pairs, per = at[name]
            f0 = ffn_base[name]
            if name not in ("in0", "in2"):
                rms_act(act, state_of[name])

            def body(i):
                units = Units(n0, i, 4)
                hi(act, units, LEAD)
                hi(act, units, LEAD + 1)
                if name == "in0" and isinstance(i, int):
                    rms_act(act, 0)
                act.wait_ge(pair_free, i * 2 + (q0 + 1))
                act.activation(buf_a[:, :, :], buf_a[:, :, :], ACT.Silu).then_inc(silu_done, 1)
                hi(act, units, LEAD + 2)
                if name == "in0" and isinstance(i, int):
                    load_consts(act)
                hi(act, units, LEAD + 3)
            ffn_steps(act, n0, body)

        def ffn_steps(eng, n0, body):
            if n0 == 0:
                body(0)
            with eng.Fori(0 if n0 else 1, FFN_STEPS) as i:
                body(i)

        def ffn_in_dve(dve, name):
            n0, q0, pairs, per = at[name]
            f0 = ffn_base[name]
            if name not in ("in0", "in2"):
                rstd_dve(dve, state_of[name])

            def body(i):
                units = Units(n0, i, 4)
                lo(dve, units, LEAD)
                lo(dve, units, LEAD + 1)
                if name == "in0" and isinstance(i, int):
                    rstd_dve(dve, 0)
                dve.wait_ge(unit_used, units.number(2))
                dve.tensor_tensor(buf_a[:, :, :], psum_pair(0), bc(rstd[:, :], 2), ALU.mult)\
                    .then_inc(pair_free, 1)
                lo(dve, units, LEAD + 2)
                lo(dve, units, LEAD + 3)
                dve.wait_ge(unit_used, units.number(4))
                dve.tensor_tensor(buf_b[:, :, :], psum_pair(1), bc(rstd[:, :], 2), ALU.mult)\
                    .then_inc(pair_free, 1)
                dve.wait_ge(pair_free, i * 2 + (q0 + 2))
                dve.wait_ge(silu_done, i + (f0 + 1))
                dve.tensor_tensor(buf_b[:, :, :], buf_b[:, :, :], buf_a[:, :, :], ALU.mult)\
                    .then_inc(hid_made, 1)
                dve.wait_ge(hid_made, i + (f0 + 1))
                two = slice(0, 2) if isinstance(i, int) else bass.ds(i * 2, 2)
                h, l = hh[:, two, :], hl[:, two, :]
                dve.tensor_copy(h, buf_b[:, :, :]).then_inc(hid_hi, 1)
                dve.wait_ge(hid_hi, i + (f0 + 1))
                dve.tensor_tensor(l, buf_b[:, :, :], h.bitcast(F32), ALU.subtract)\
                    .then_inc(hid_ready, 1)
            ffn_steps(dve, n0, body)
            if name == "in0":
                keep_consts(dve)

        def ffn_out_ready(pe, name):
            f0 = ffn_base["in" + name[3:]]

            def ready(u):
                need = min(2 * u + 2, FFN_STEPS)
                pe.wait_ge(hid_ready, f0 + need)
            return ready

        eps_col = rest.tile("eps_col", [P, 1])
        zero_col = rest.tile("zero_col", [P, 1])

        w_ssm = t["ssm_w_in"][0]

        def squares_of(buffer):
            return buffer[:, :, :].rearrange("p (o c) s -> p o (c s)", o=2)

        class Slot:

            def __init__(self, i, s0):
                self.i, self.s0, self.par = i, s0, s0 % 2
                self.units = Units(at["ssm"][0] + 6 * s0, i, 12) if "ssm" in at else None
                self.last = s0 == GROUPS
                self.segm, self.cumb, self.xdt, self.xde, self.btok = \
                    scan_last if s0 == GROUPS else scan_main
                self.ysq = squares_of((scan_last if s0 == GROUPS + 1 else scan_main)[3])

            def count(self, k=0):
                return self.i * 2 + (self.s0 + k)

            def pairs(self, k):
                return self.i * 6 + (at["ssm"][1] + 3 * self.s0 + k)

            def first(self, k):
                return isinstance(self.i, int) and self.s0 - k < 0

        def slots(eng, slot, tail=True):
            slot(Slot(0, 0))
            slot(Slot(0, 1))
            with eng.Fori(0, 3) as i:
                slot(Slot(i, 2))
                slot(Slot(i, 3))
            if tail:
                slot(Slot(0, 8))
                slot(Slot(0, 9))

        def sout_units():
            return Units(at["sout"][0], 0, 0)

        def has(s, k):
            return not isinstance(s.i, int) or 0 <= s.s0 - k < GROUPS

        def ssm_pe(pe):
            n0, q0, _, _ = at["ssm"]

            def unit(s, u):
                if not has(s, 0):
                    return
                if u % 2 == 0:
                    pe.wait_ge(pair_free, s.pairs(u // 2 - 1))
                j = (3 * s.s0 + u // 2) % 2
                if u < 4:
                    if isinstance(s.i, int) and s.s0 == 0 and u < 2:
                        pe.wait_ge(x_split, splits_before["ssm"] - X_PAIRS + 2 * u + 2)
                    products(pe, s.units, u, psum_pair(j), k_views(4 * (u % 2), 4, KD), u % 2 == 1,
                             xh, xl)
                else:
                    views = [(u - 4, [(k, k == 0, k * P, k == KD - 1) for k in range(KD)])]
                    products(pe, s.units, u, psum_pair(j), views, u == 5, xh, xl)

            def dt_product():
                pe.wait_ge(wdt_ready, 1)
                for k in range(KD):
                    pe.matmul(pa[:, 2, :], wdt_hi[:, k, :], xh[:, k, :], start=k == 0, stop=False)
                    pe.matmul(pa[:, 2, :], wdt_hi[:, k, :], xl[:, k, :], start=False, stop=False)
                    l = pe.matmul(pa[:, 2, :], wdt_lo[:, k, :], xh[:, k, :], start=False, stop=k == KD - 1)
                l.then_inc(dt_used, 1)

            def dt_turn():
                pe.wait_ge(cum_ready, 1)
                idn = ident[DT0:P, DT0:P]
                for c in range(NC):
                    for v, src in ((0, dt_c), (1, dt_t)):
                        l = pe.transpose(pa[:, 2, (v * NC + c) * HEADS:(v * NC + c + 1) * HEADS],
                                         src[DT0:P, c * L:(c + 1) * L], idn)
                l.then_inc(tok_turned, 1)

            def part_a(s):
                pe.wait_ge(conv_done, s.count())
                if not s.first(2):
                    pe.wait_ge(y_gated, s.count(-1))
                for c in range(NC):
                    for j in range(2):
                        o = (c % 2) * 256 + j * P
                        pe.transpose(pa[:, c // 2, o:o + P], xv[1 - s.par][:, j, c * L:(c + 1) * L],
                                     ident[:, :])
                for c in range(NC):
                    l = pe.transpose(pa[:, 2, c * P:(c + 1) * P], bcv[:, 0, c * L:(c + 1) * L],
                                     ident[:, :])
                l.then_inc(turned_a, 1)

            def part_cb(s):
                if not s.first(2):
                    pe.wait_ge(y_final, s.count(-1))
                for c in range(NC):
                    l = pe.matmul(pa[:, 3, c * L:(c + 1) * L], bcv[:, 0, c * L:(c + 1) * L],
                                  bcv[:, 1, c * L:(c + 1) * L], start=True, stop=True)
                l.then_inc(cb_product, 1)

            def part_b(s):
                pe.wait_ge(xde_ready, s.count())
                pe.wait_ge(btok_ready, s.count())
                pe.wait_ge(cbm_ready, s.count())
                for c in range(NC - 1):
                    o = (c % 2) * 256
                    l = pe.matmul(pa[:, 2 + c // 2, o:o + 256], s.btok[:, c, :], s.xde[:, c, :],
                                  start=True, stop=True)
                l.then_inc(states_product, 1)

            def part_c(s):
                pe.wait_ge(m_ready, s.count())
                pe.wait_ge(c_ready, s.count())
                pe.wait_ge(xdt_ready, s.count())
                pe.wait_ge(prev_step, s.count() * 5)
                for h in range(HG):
                    for c in range(NC):
                        out = pa[64 * (h % 2):64 * (h % 2) + HP, h // 2, c * L:(c + 1) * L]
                        l = pe.matmul(out, s.xdt[:, c, h * HP:(h + 1) * HP], s.segm[:, h, c * L:(c + 1) * L],
                                      start=True, stop=c == 0)
                        if c:
                            l = pe.matmul(out, prev[:, c - 1, h * HP:(h + 1) * HP],
                                          s.cumb[:, h, c * L:(c + 1) * L], start=False, stop=True)
                l.then_inc(y_product, 1)

            def sout(first, count):
                for n in range(first, first + count):
                    r, u = SOUT_ORDER[n]
                    if u == 0:
                        pe.wait_ge(pair_free, at["sout"][1] + r - 1)
                    pe.wait_ge(y_split, 2 * u + 2)
                    products(pe, sout_units(), n, psum_pair(r), k_views(UK * u, UK, KI), u == 3,
                             y_hi, y_lo)

            def y_sums(s):
                pe.wait_ge(y_halved, s.count(-1))
                token_sums(pe, s.ysq[:, 0, :], y_stat)

            def y_spreads(s):
                pe.wait_ge(y_inv, s.count(-1))
                spread_rows(pe, yinv, y_spread)

            def slot(s):
                unit(s, 0)
                if isinstance(s.i, int) and s.s0 == 0:
                    stats(pe, state_of["ssm"])
                if has(s, 2):
                    y_sums(s)
                unit(s, 1)
                if isinstance(s.i, int) and s.s0 == 0:
                    spread_stats(pe, state_of["ssm"])
                if has(s, 2):
                    y_spreads(s)
                if has(s, 1):
                    part_a(s)
                unit(s, 2)
                if has(s, 1):
                    part_cb(s)
                unit(s, 3)
                if isinstance(s.i, int) and s.s0 == 0:
                    dt_product()
                if has(s, 1):
                    part_b(s)
                unit(s, 4)
                if has(s, 1):
                    part_c(s)
                unit(s, 5)
                if isinstance(s.i, int) and s.s0 == 0:
                    dt_turn()
            slots(pe, slot, tail=False)
            s = Slot(0, GROUPS)
            sout(0, 1)
            y_sums(s)
            sout(1, 1)
            y_spreads(s)
            part_a(s)
            part_cb(s)
            sout(2, 1)
            part_b(s)
            sout(3, 1)
            part_c(s)
            s = Slot(0, GROUPS + 1)
            sout(4, 1)
            y_sums(s)
            y_spreads(s)
            sout(5, 3)


        def ssm_act(act):
            n0 = at["ssm"][0]
            act.wait_ge(unit_used, n0)
            act.dma_start(wdt[:, :, :], w_ssm.rearrange("(k p) c -> p k c", p=P)[:, :, 6176 - P:6176])\
                .then_inc(wdt_loaded, 16)
            d = slice(DT0, P)

            def dt_steps():
                act.wait_ge(dt_v, 1)
                act.activation(dt_e[d, :], dt_raw[d, :], ACT.Abs).then_inc(dt_s, 1)
                act.wait_ge(dt_s, 1)
                act.wait_ge(ssm_consts, 16 * 4)
                act.activation(dt_e[d, :], dt_e[d, :], ACT.Exp, scale=-1.0).then_inc(dt_s, 1)
                act.activation(a_neg[d, :], a_neg[d, :], ACT.Exp).then_inc(dt_s, 1)
                act.wait_ge(dt_v, 2)
                act.activation(dt_ln[d, :], dt_u[d, :], ACT.Ln).then_inc(dt_s, 1)

            def base(s, group, pre, out, col, done):
                for tt in range(2):
                    act.activation(out[:, tt, :], pre[:, tt, 3:3 + S], ACT.Identity,
                                   bias=gcw[group][:, 4, col + tt:col + tt + 1],
                                   scale=gcw[group][:, 3, col + tt:col + tt + 1]).then_inc(done, 1)

            def y_root(s):
                act.wait_ge(y_stat, s.count(-1))
                act.activation(yrms[:, :], pa[:, 3, 0:NC], ACT.Sqrt, bias=eps_col[:, :],
                               scale=1.0 / 256).then_inc(y_rms, 1)

            def y_hi_of(b):
                act.wait_ge(y_final, b + 1)
                if b < 4:
                    act.wait_ge(y_product, GROUPS - 1)
                elif b < 6:
                    act.wait_ge(y_stat, GROUPS - 1)
                act.activation(y_hi[:, 2 * b:2 * b + 2, :], y32[:, 2 * b:2 * b + 2, :], ACT.Copy)\
                    .then_inc(yhi_ready, 1)

            def slot(s):
                if s.last:
                    y_hi_of(0)
                    y_hi_of(1)
                if has(s, 0) or s.last:
                    hi(act, s.units, LEAD)
                if isinstance(s.i, int) and s.s0 == 0:
                    rms_act(act, state_of["ssm"])
                if has(s, 1):
                    act.wait_ge(params_ready, s.count() * 5)
                    act.wait_ge(pair_free, s.pairs(0))
                    base(s, 1 - s.par, pre_bc, bcv, 2, conv_base_bc)
                    if s.last:
                        y_hi_of(2)
                        y_hi_of(3)
                    act.wait_ge(cum_stored, 16)
                    if isinstance(s.i, int) and s.s0 == 1:
                        act.wait_ge(tok_ready, 1)
                    if isinstance(s.i, int) and s.s0 == GROUPS:
                        act.wait_ge(unit_used, s.units.number(0))
                    elif not s.first(2):
                        act.wait_ge(y_product, s.count(-1))
                    rows = cum_dram[bass.ds(s.count(-1) * HG, HG), :]
                    act.dma_start(s.cumb[:, :, :], rows.partition_broadcast(P)).then_inc(cum_loaded, 16)
                    if s.last:
                        y_root(s)
                    act.wait_ge(conv_tap_bc, s.count() * 6)
                    act.activation(tanh[:, 2:4, :], bcv[:, :, :], ACT.Tanh).then_inc(conv_tanh_bc, 1)
                if has(s, 0) or s.last:
                    hi(act, s.units, LEAD + 1)
                if has(s, 2) and not s.last:
                    y_root(s)
                if has(s, 1):
                    act.wait_ge(dte_diff, s.count())
                    act.activation(dte[:, :, :], dte[:, :, :], ACT.Exp).then_inc(dte_ready, 1)
                    act.wait_ge(seg_ready, s.count() * 16)
                    act.activation(s.segm[:, :, :], s.segm[:, :, :], ACT.Exp).then_inc(decay_ready, 1)
                if s.last:
                    hi(act, s.units, LEAD + 2)
                    y_hi_of(4)
                    y_hi_of(5)
                if has(s, 0):
                    hi(act, s.units, LEAD + 2)
                    act.wait_ge(pair_free, s.pairs(1))
                    zb = (buf_a, buf_b)[s.par]
                    act.activation(tanh[:, 0:2, :], zb[:, :, :], ACT.Tanh, scale=0.5).then_inc(z_tanh, 1)
                if has(s, 1):
                    act.activation(s.cumb[:, :, :], s.cumb[:, :, :], ACT.Exp).then_inc(growth_ready, 1)
                    act.wait_ge(turned_a, s.count())
                    act.activation(s.btok[:, :, :], pa[:, 2, :], ACT.Copy).then_inc(btok_ready, 1)
                if isinstance(s.i, int) and s.s0 == 0:
                    act.wait_ge(wdt_loaded, 16)
                    act.activation(wdt_hi[:, :, :], wdt[:, :, :], ACT.Copy).then_inc(wdt_hi_ready, 1)
                if has(s, 0):
                    hi(act, s.units, LEAD + 3)
                    hi(act, s.units, LEAD + 4)
                    act.wait_ge(params_ready, s.count(1) * 5)
                    act.wait_ge(pair_free, s.pairs(2))
                    base(s, s.par, pre_x, xv[s.par], 0, conv_base_x)
                if isinstance(s.i, int) and s.s0 == 0:
                    dt_steps()
                if has(s, 0):
                    hi(act, s.units, LEAD + 5)
                    act.wait_ge(conv_tap_x, s.count(1) * 6)
                    act.wait_ge(z_ready, s.count(1))
                    act.activation(tanh[:, 0:2, :], xv[s.par][:, :, :], ACT.Tanh).then_inc(conv_tanh_x, 1)
                if s.last:
                    hi(act, s.units, LEAD + 3)
                    hi(act, s.units, LEAD + 4)
                    y_hi_of(6)
                if has(s, 1):
                    act.wait_ge(y_gated, s.count())
                    act.activation(squares_of(s.xde), y32[:, bass.ds(s.count(-1) * 2, 2), :],
                                   ACT.Square).then_inc(y_squared, 1)
                if isinstance(s.i, int) and s.s0 == 0:
                    act.wait_ge(cum_ready, 1)
                    act.dma_start(cum_dram, dt_c[DT0:P, :]).then_inc(cum_stored, 16)
            slots(act, slot)
            units = sout_units()
            hi(act, units, LEAD + 5)
            y_hi_of(7)
            hi(act, units, LEAD + 6)
            sq_act(act, state_of["sout"] + 1, 0, at["sout"][1])
            hi(act, units, LEAD + 7)
            sq_act(act, state_of["sout"] + 1, 1, at["sout"][1] + 1)

        def ssm_dve(dve):
            n0, q0, _, _ = at["ssm"]
            d = slice(DT0, P)

            def dt_steps():
                dve.wait_ge(dt_used, 1)
                dve.tensor_tensor(dt_raw[d, :], pa[d, 2, :], rstd[d, :], ALU.mult).then_inc(cum_ready_v, 1)
                dve.wait_ge(cum_ready_v, 1)
                dve.wait_ge(ssm_consts, 16 * 4)
                dve.tensor_scalar(dt_raw[d, :], dt_raw[d, :], dt_bias[d, :], None, ALU.add).then_inc(dt_v, 1)
                dve.wait_ge(dt_s, 2)
                dve.tensor_scalar(dt_u[d, :], dt_e[d, :], 1.0, None, ALU.add).then_inc(dt_v, 1)
                dve.wait_ge(dt_v, 2)
                dve.reciprocal(dt_r[d, :], dt_u[d, :]).then_inc(dt_v, 1)
                dve.scalar_tensor_tensor(dt_t[d, :], dt_u[d, :], 1.0, dt_e[d, :], ALU.subtract,
                                         ALU.subtract).then_inc(dt_v, 1)
                dve.wait_ge(dt_v, 4)
                dve.scalar_tensor_tensor(dt_c[d, :], dt_t[d, :], -1.0, dt_r[d, :], ALU.mult,
                                         ALU.mult).then_inc(dt_v, 1)
                dve.wait_ge(dt_v, 5)
                dve.wait_ge(dt_s, 4)
                dve.tensor_tensor(dt_u[d, :], dt_c[d, :], dt_ln[d, :], ALU.add).then_inc(dt_v, 1)
                dve.wait_ge(dt_v, 6)
                dve.scalar_tensor_tensor(dt_t[d, :], dt_raw[d, :], 0.0, dt_u[d, :], ALU.max,
                                         ALU.add).then_inc(dt_v, 1)
                dve.wait_ge(dt_v, 7)
                dve.tensor_scalar(dt_r[d, :], dt_t[d, :], a_neg[d, :], -1.0, ALU.mult, ALU.mult)\
                    .then_inc(dt_v, 1)
                dve.wait_ge(dt_v, 8)
                for c in range(NC):
                    l = dve.tensor_tensor_scan(dt_c[d, c * L:(c + 1) * L], ones[d, :],
                                               dt_r[d, c * L:(c + 1) * L], 0.0, ALU.mult, ALU.add)
                l.then_inc(cum_ready, 1)

            def conv(s, k_group, group, pre, out, col, base_done, tapped):
                for n, k in enumerate((2, 1, 0)):
                    for tt in range(2):
                        if k == 2:
                            dve.wait_ge(base_done, k_group * 2 + (tt + 1))
                        else:
                            dve.wait_ge(tapped, k_group * 6 + (2 * n + tt - 1))
                        dve.scalar_tensor_tensor(out[:, tt, :], pre[:, tt, k:k + S],
                                                 gcw[group][:, k, col + tt:col + tt + 1], out[:, tt, :],
                                                 ALU.mult, ALU.add).then_inc(tapped, 1)

            def y_reciprocal(s):
                dve.wait_ge(y_rms, s.count(-1))
                dve.reciprocal(yinv[:, :], yrms[:, :]).then_inc(y_inv, 1)

            def y_scale(s):
                dve.wait_ge(y_spread, s.count(-1))
                for j in range(2):
                    yt = y32[:, bass.ds(s.count(-2) * 2 + j, 1), :].squeeze(1)
                    ins = dve.scalar_tensor_tensor(yt, yt, gdn[s.par][:, 1, j:j + 1], pa[:, 3, :],
                                                   ALU.mult, ALU.mult)
                ins.then_inc(y_final, 1)

            def y_lo_of(b):
                dve.wait_ge(yhi_ready, b + 1)
                dve.tensor_tensor(y_lo[:, 2 * b:2 * b + 2, :], y32[:, 2 * b:2 * b + 2, :],
                                  y_hi[:, 2 * b:2 * b + 2, :].bitcast(F32), ALU.subtract)\
                    .then_inc(y_split, 1)

            def slot(s):
                if s.last:
                    y_lo_of(0)
                    y_lo_of(1)
                if has(s, 1):
                    dve.wait_ge(unit_used, s.units.number(0))
                    dve.tensor_tensor(pre_bc[:, :, 3:3 + S], psum_pair(3 * s.s0 - 1), bc(rstd[:, :], 2),
                                      ALU.mult).then_inc(pair_free, 1)
                if has(s, 0) or s.last:
                    lo(dve, s.units, LEAD)
                if s.last:
                    y_lo_of(2)
                    y_lo_of(3)
                if isinstance(s.i, int) and s.s0 == 0:
                    rstd_dve(dve, state_of["ssm"])
                if has(s, 1):
                    conv(s, s.count(-1), 1 - s.par, pre_bc, bcv, 2, conv_base_bc, conv_tap_bc)
                if s.last:
                    y_reciprocal(s)
                if has(s, 1):
                    dve.wait_ge(conv_tanh_bc, s.count())
                    dve.scalar_tensor_tensor(bcv[:, :, :], tanh[:, 2:4, :], 1.0, bcv[:, :, :], ALU.add,
                                             ALU.mult).then_inc(conv_done, 1)
                if has(s, 0) or s.last:
                    lo(dve, s.units, LEAD + 1)
                if has(s, 2) and not s.last:
                    y_reciprocal(s)
                if s.last:
                    y_scale(s)
                if has(s, 1):
                    if isinstance(s.i, int) and s.s0 == 1:
                        dve.wait_ge(tok_ready, 1)
                    dve.tensor_copy(gtok[:, :, :, :], tok_all[:, :, :, bass.ds(s.count(-1) * HG, HG)])\
                        .then_inc(gtok_ready, 1)
                    dve.wait_ge(gtok_ready, s.count())
                    dve.wait_ge(cum_loaded, s.count() * 16)
                    ends = s.cumb[:, :, :].rearrange("p h (c l) -> p c h l", l=L)[:, :, :, L - 1]
                    dve.tensor_tensor(dte[:, :, :], ends, gtok[:, 0, :, :], ALU.subtract)\
                        .then_inc(dte_diff, 1)
                    for h in range(HG):
                        for c in range(NC):
                            dve.tensor_scalar(s.segm[:, h, c * L:(c + 1) * L],
                                              s.cumb[:, h, c * L:(c + 1) * L],
                                              gtok[:, 0, c, h:h + 1], 0.0, ALU.subtract, ALU.min)\
                                .then_inc(seg_ready, 1)
                if has(s, 0):
                    zb = (buf_a, buf_b)[s.par]
                    dve.wait_ge(unit_used, s.units.number(2))
                    dve.tensor_tensor(zb[:, :, :], psum_pair(3 * s.s0), bc(rstd[:, :], 2), ALU.mult)\
                        .then_inc(pair_free, 1)
                if has(s, 2) and not s.last:
                    y_scale(s)
                if has(s, 0):
                    lo(dve, s.units, LEAD + 2)
                if has(s, 1):
                    dve.wait_ge(turned_a, s.count())
                    dve.tensor_tensor(
                        s.xdt[:, :, :].rearrange("p c (h q) -> p (c h) q", h=HG),
                        pa[:, 0:2, :].rearrange("p b (m q) -> p (b m) q", q=HP),
                        gtok[:, 1, :, :].rearrange("p c h -> p (c h)").unsqueeze(2)
                        .broadcast_to((P, NC * HG, HP)), ALU.mult).then_inc(xdt_ready, 1)
                if has(s, 1):
                    dve.wait_ge(dte_ready, s.count())
                    dve.wait_ge(xdt_ready, s.count())
                    dve.tensor_tensor(
                        s.xde[:, :, :].rearrange("p c (h q) -> p (c h) q", h=HG),
                        s.xdt[:, :, :].rearrange("p c (h q) -> p (c h) q", h=HG),
                        dte[:, :, :].rearrange("p c h -> p (c h)").unsqueeze(2)
                        .broadcast_to((P, NC * HG, HP)), ALU.mult).then_inc(xde_ready, 1)
                    dve.wait_ge(growth_ready, s.count())
                    dve.tensor_copy(cd[:, :, :], s.cumb[:, :, :].rearrange("p h (c l) -> p h c l", l=L)
                                    [:, :, :, L - 1]).then_inc(cd_ready, 1)
                    dve.wait_ge(cb_product, s.count())
                    dve.tensor_tensor(cbm[:, :].rearrange("p (c l) -> p c l", c=NC),
                                      pa[:, 3, :].rearrange("p (c l) -> p c l", c=NC),
                                      bc(mask[:, :], NC), ALU.mult).then_inc(cbm_ready, 1)
                    dve.wait_ge(cbm_ready, s.count())
                    dve.wait_ge(decay_ready, s.count())
                    dve.tensor_tensor(s.segm[:, :, :], s.segm[:, :, :], bc(cbm[:, :], HG), ALU.mult)\
                        .then_inc(m_ready, 1)
                if isinstance(s.i, int) and s.s0 == 0:
                    dve.wait_ge(wdt_hi_ready, 1)
                    dve.tensor_tensor(wdt_lo[:, :, :], wdt[:, :, :], wdt_hi[:, :, :].bitcast(F32),
                                      ALU.subtract).then_inc(wdt_ready, 1)
                if s.last:
                    lo(dve, s.units, LEAD + 2)
                    y_lo_of(4)
                    y_lo_of(5)
                if has(s, 0):
                    lo(dve, s.units, LEAD + 3)
                    dve.wait_ge(unit_used, s.units.number(4))
                    dve.tensor_tensor(pre_x[:, :, 3:3 + S], psum_pair(3 * s.s0 + 1), bc(rstd[:, :], 2),
                                      ALU.mult).then_inc(pair_free, 1)
                    lo(dve, s.units, LEAD + 4)
                if isinstance(s.i, int) and s.s0 == 0:
                    dt_steps()
                if has(s, 1):
                    dve.wait_ge(states_product, s.count())
                    step = 0
                    for c in range(NC - 1):
                        src = pa[:, 2 + c // 2, (c % 2) * 256:(c % 2) * 256 + 256]
                        if c == 0:
                            dve.tensor_copy(prev[:, 0, :], src).then_inc(prev_step, 1)
                            step += 1
                            continue
                        dve.wait_ge(prev_step, s.count(-1) * 5 + step)
                        dve.tensor_tensor(prev[:, c, :].rearrange("p (h q) -> p h q", h=HG),
                                          prev[:, c - 1, :].rearrange("p (h q) -> p h q", h=HG),
                                          cd[:, :, c:c + 1].broadcast_to((P, HG, HP)), ALU.mult)\
                            .then_inc(prev_step, 1)
                        step += 1
                        dve.wait_ge(prev_step, s.count(-1) * 5 + step)
                        dve.tensor_tensor(prev[:, c, :], prev[:, c, :], src, ALU.add)\
                            .then_inc(prev_step, 1)
                        step += 1
                if has(s, 0):
                    conv(s, s.count(), s.par, pre_x, xv[s.par], 0, conv_base_x, conv_tap_x)
                    lo(dve, s.units, LEAD + 5)
                    dve.wait_ge(conv_tanh_x, s.count(1))
                    dve.scalar_tensor_tensor(xv[s.par][:, :, :], tanh[:, 0:2, :], 1.0, xv[s.par][:, :, :],
                                             ALU.add, ALU.mult)
                if s.last:
                    lo(dve, s.units, LEAD + 3)
                    lo(dve, s.units, LEAD + 4)
                    y_lo_of(6)
                if has(s, 1):
                    dve.wait_ge(y_product, s.count())
                    for j in range(2):
                        yt = y32[:, bass.ds(s.count(-1) * 2 + j, 1), :].squeeze(1)
                        dve.scalar_tensor_tensor(yt, xv[1 - s.par][:, j, :],
                                                 gdn[1 - s.par][:, 0, j:j + 1], pa[:, j, :],
                                                 ALU.mult, ALU.add).then_inc(y_plus, 1)
                    dve.wait_ge(y_plus, s.count() * 2)
                    dve.wait_ge(z_ready, s.count())
                    yp = y32[:, bass.ds(s.count(-1) * 2, 2), :]
                    dve.scalar_tensor_tensor(yp, yp, 0.5, (buf_a, buf_b)[1 - s.par][:, :, :], ALU.mult,
                                             ALU.mult).then_inc(y_gated, 1)
                if isinstance(s.i, int) and s.s0 == 0:
                    dve.wait_ge(tok_turned, 1)
                    dve.tensor_copy(tok_all[:, :, :, :], pa[:, 2, 0:2 * NC * HEADS]).then_inc(tok_ready, 1)
            slots(dve, slot)
            units = sout_units()
            lo(dve, units, LEAD + 5)
            y_lo_of(7)
            lo(dve, units, LEAD + 6)
            residual(dve, "sout", 0, 0, units.number(7), 1.0, gain_after("sout"))
            lo(dve, units, LEAD + 7)
            residual(dve, "sout", 0, 1, units.number(8), 1.0, gain_after("sout"))

        def ssm_pool(pool):
            n0 = at["ssm"][0]
            pool.wait_ge(unit_used, n0)
            pool.memset(pre_x[:, :, 0:3], 0.0).then_inc(halo_ready, 1)
            pool.memset(pre_bc[:, :, 0:3], 0.0).then_inc(halo_ready, 1)
            pool.wait_ge(cw_ready, 2)
            pool.wait_ge(gains_ready, 1)
            pool.wait_ge(ssm_consts, 16 * 4)

            def group(s):
                g, r = s.count(), s.par
                if not s.first(2):
                    pool.wait_ge(y_final, s.count(-1))
                for dst, src in ((gcw[r][:, :, 0:2], cw[:, :, bass.ds(g * 2, 2)]),
                                 (gcw[r][:, :, 2:3], cw[:, :, bass.ds(g + 16, 1)]),
                                 (gcw[r][:, :, 3:4], cw[:, :, bass.ds(g + 24, 1)]),
                                 (gdn[r][:, 0, :], dskip[:, bass.ds(g * 2, 2)]),
                                 (gdn[r][:, 1, :], gains[:, bass.ds(g * 2 + G["ssm_norm"], 2)])):
                    pool.tensor_copy(dst, src).then_inc(params_ready, 1)

            def slot(s):
                if has(s, 2):
                    pool.wait_ge(y_squared, s.count(-1))
                    pool.tensor_tensor(s.ysq[:, 0, :], s.ysq[:, 0, :], s.ysq[:, 1, :], ALU.add)\
                        .then_inc(y_halved, 1)
                if has(s, 0):
                    group(s)
                    zb = (buf_a, buf_b)[s.par]
                    pool.wait_ge(z_tanh, s.count(1))
                    pool.tensor_tensor(tanh[:, 0:2, :], tanh[:, 0:2, :], zb[:, :, :], ALU.mult)\
                        .then_inc(z_product, 1)
                    pool.wait_ge(z_product, s.count(1))
                    pool.tensor_tensor(zb[:, :, :], tanh[:, 0:2, :], zb[:, :, :], ALU.add)\
                        .then_inc(z_ready, 1)
                if has(s, 1):
                    pool.wait_ge(cd_ready, s.count())
                    pool.wait_ge(conv_done, s.count())
                    pool.tensor_tensor(s.cumb[:, :, :], s.cumb[:, :, :], bc(bcv[:, 1, :], HG), ALU.mult)\
                        .then_inc(c_ready, 1)
            slots(pool, slot)

        def ssm_sp(sp):
            def slot(s):
                if not has(s, 0):
                    return
                g = s.count()
                for u in range(4):
                    load(sp, s.units, u, row_unit(w_ssm, UK * (u % 2), UK, g * 256 + (u // 2) * DI))
                for u in range(2):
                    src = w_ssm.rearrange("(k p) c -> p k c", p=P)[
                        :, :, bass.ds(g * P + (2 * DI + u * GROUPS * NST), P)]
                    load(sp, s.units, 4 + u, src, wide=P)
            slots(sp, slot)


        class PairSlot:
            def __init__(self, name, i, s0):
                self.i, self.s0, self.name = i, s0, name
                self.n0, self.q0, self.pairs, _ = at[name]
                self.units = Units(self.n0 + 2 * s0, i, 4)
                self.turn = name == "kv" and s0 > 4
                self.work = not isinstance(i, int) or s0 < self.pairs
                self.before = 0 if name == "kv" else at["kv"][2]
                self.ropes_before = 0 if name == "kv" else 4

            def count(self, k=0):
                return self.i * 2 + (self.s0 + k)

            def done(self, k=0):
                return self.i * 2 + (self.s0 + self.before + k)

            def roped(self, k=0):
                return self.i * 2 + (self.s0 + self.ropes_before + k)

        def pair_slots(eng, name, slot):
            slot(PairSlot(name, 0, 0))
            if name == "kv":
                with eng.Fori(0, 2) as i:
                    slot(PairSlot(name, i, 1))
                    slot(PairSlot(name, i, 2))
                rest_of = range(5, 9)
            else:
                rest_of = range(1, 5)
            for s0 in rest_of:
                slot(PairSlot(name, 0, s0))

        def rotate(pe, s):
            pe.wait_ge(pair_free, s.count(s.q0))
            if s.s0 == 1:
                pe.wait_ge(rope_loaded, 16 * 3 * (2 if s.name == "q" else 1))
            if s.turn:
                for c in range(NC):
                    for o in range(2):
                        w0 = (c % 2) * 256 + o * P
                        l = pe.transpose(pa[:, c // 2, w0:w0 + P], buf_a[:, o, c * P:(c + 1) * P],
                                         ident[:, :])
            else:
                for o in range(2):
                    l = pe.matmul(pa[:, o, :], rot[:, :], buf_a[:, o, :], start=True, stop=True)
            l.then_inc(head_rotated, 1)

        def pair_pe(pe, name):
            def slot(s):
                par = s.s0 % 2
                for u in range(2):
                    if s.work:
                        if u == 0:
                            pe.wait_ge(pair_free, s.count(s.q0 - 1))
                        if s.s0 == 0:
                            pe.wait_ge(x_split, splits_before[name] - X_PAIRS + 2 * u + 2)
                        products(pe, s.units, u, psum_pair(par), k_views(4 * u, 4, KD), u == 1, xh, xl)
                    if s.s0 == 0:
                        (stats, spread_stats)[u](pe, state_of[name])
                    elif u == 0 and not (name == "kv" and not s.work):
                        if name == "q" and not s.work:
                            pe.wait_ge(pair_free, s.count(s.q0 - 1))
                            logits(pe, Step(0, 0))
                        rotate(pe, s)
            pair_slots(pe, name, slot)

        def pair_act(act, name):
            dram = q_dram if name == "q" else k_dram

            def slot(s):
                if s.work:
                    hi(act, s.units, LEAD)
                if s.s0 == 0:
                    if name == "kv":
                        for r in range(2):
                            act.sem_inc(heads_stored[r], 16)
                        act.wait_ge(unit_used, s.n0)
                    else:
                        act.wait_ge(unit_used, s.n0)
                    for dst, src in ((cos_t, t["rope_tables"][0]), (sin_t, t["rope_tables"][1]),
                                     (rot, t["rope_rotation"])):
                        act.dma_start(dst[:, :], src).then_inc(rope_loaded, 16)
                    rms_act(act, state_of[name])
                if s.work:
                    hi(act, s.units, LEAD + 1)
                if name == "q" and not s.work:
                    exps(act, Step(0, 0))
                if s.s0:
                    act.wait_ge(heads_ready, s.done())
                    d = v_dram if s.turn else dram
                    h0 = s.count(-1) * 2 - (8 if s.turn else 0)
                    par = (s.s0 - 1) % 2
                    act.dma_start(d[bass.ds(h0, 2)].rearrange("o p x -> p o x"),
                                  heads_out[par][:, :, :]).then_inc(heads_stored[par], 16)
            pair_slots(act, name, slot)

        def pair_dve(dve, name):
            def slot(s):
                resplit = name == "kv" and not s.work
                if resplit:
                    dve.wait_ge(unit_used, s.units.number(0) - 1)
                    for p in range(2):
                        split_x(dve, splits_before["in2"] - X_PAIRS, p, gain_after("kv"))
                if s.s0:
                    dve.wait_ge(unit_used, s.units.number(0))
                    dve.scalar_tensor_tensor(buf_a[:, :, :], psum_pair(s.s0 - 1),
                                             SCALE if name == "q" else 1.0, bc(rstd[:, :], 2),
                                             ALU.mult, ALU.mult).then_inc(pair_free, 1)
                if name == "q" and not s.work:
                    row_max(dve, Step(0, 0))
                if resplit:
                    for p in range(2, X_PAIRS):
                        split_x(dve, splits_before["in2"] - X_PAIRS, p, gain_after("kv"))
                if s.work:
                    lo(dve, s.units, LEAD)
                if s.s0 == 0:
                    rstd_dve(dve, state_of[name])
                    dve.wait_ge(rope_loaded, 16 * 3 * (2 if name == "q" else 1))
                if s.s0:
                    par = (s.s0 - 1) % 2
                    if not s.turn:
                        dve.wait_ge(pair_free, s.count(s.q0))
                        dve.tensor_tensor(buf_b[:, :, :], buf_a[:, :, :], bc(cos_t[:, :], 2), ALU.mult)\
                            .then_inc(rope_cos, 1)
                    if isinstance(s.i, int):
                        dve.wait_ge(heads_stored[par], 16 * ((s.done(-1) + 1 - par) // 2 + 1))
                    else:
                        dve.wait_ge(heads_stored[par], (s.i + 1) * 16)
                    dve.wait_ge(head_rotated, s.done())
                    if s.turn:
                        dve.tensor_copy(
                            heads_out[par][:, :, :].rearrange("p o (c e) -> p o c e", e=P),
                            pa[:, 0:2, :].rearrange("p b (c o e) -> p o (b c) e", c=2, o=2))\
                            .then_inc(heads_ready, 1)
                    else:
                        dve.tensor_tensor(heads_out[par][:, :, :], pa[:, 0:2, :], bc(sin_t[:, :], 2),
                                          ALU.mult).then_inc(rope_sin, 1)
                        dve.wait_ge(rope_sin, s.roped())
                        dve.tensor_tensor(heads_out[par][:, :, :], heads_out[par][:, :, :],
                                          buf_b[:, :, :], ALU.add).then_inc(heads_ready, 1)
                if s.work:
                    lo(dve, s.units, LEAD + 1)
            pair_slots(dve, name, slot)
            if name == "kv":
                for r in range(2):
                    dve.wait_ge(heads_stored[r], 16 * 5)

        def pair_sp(sp, name, w):
            n0, q0, pairs, _ = at[name]
            with sp.Fori(0, pairs // 2) as i:
                units = Units(n0, i, 4)
                for r in range(2):
                    for u in range(2):
                        load(sp, units, 2 * r + u, row_unit(w, UK * u, UK, i * 512 + r * 256))


        class Step:
            def __init__(self, i, u):
                self.i, self.u0, self.u = i, u, u % 8
                self.first = u % 4 == 0
                self.q = u % 4
                self.h = (u % 8) // 4
                self.n = (self.q + 1) * P
                self.par = u % 2

            def count(self, k=0):
                return self.i * 8 + (self.u0 + k)

            def head(self, k=0):
                return self.i * 2 + (self.u0 // 4 + k)

            def exists(self):
                return not isinstance(self.i, int) or 0 <= self.i * 8 + self.u0 < AH * NC

        SUMS = 3 * P

        def att_bodies(eng, body):
            body(0)
            with eng.Fori(1, 3) as i:
                body(i)
            body(3)

        def logits(pe, s):
            if not s.exists():
                return
            if s.first:
                pe.wait_ge(head_loaded[s.h], s.i * 48 + 48 * ((s.u0 // 8) + 1))
            if not (isinstance(s.i, int) and s.count() < 2):
                pe.wait_ge(exp_ready, s.count(-1) * 2)
            for m in range(2):
                d = slice(m * HP, (m + 1) * HP)
                l = pe.matmul(pw[:, 2 * s.par + m, 0:s.n], q_cur[s.h][d, s.q * P:(s.q + 1) * P],
                              k_cur[s.h][d, 0:s.n], start=True, stop=True)
            l.then_inc(logits_ready, 1)

        def att_pe(pe):
            def head_sums(s):
                if not s.exists():
                    return
                h = s.head()
                pe.wait_ge(o_squared, s.head(1))
                for c in range(NC):
                    out = pa[:, 0, SUMS + h * NC + c:SUMS + h * NC + c + 1] if isinstance(h, int) \
                        else pa[:, 0, bass.ds(h * NC + (SUMS + c), 1)]
                    l = pe.matmul(out, buf_b[:, s.h, c * P:(c + 1) * P], ones[:, 0:1], start=True, stop=True)
                l.then_inc(o_summed, 1)

            def turn(s):
                pe.wait_ge(w_ready, s.count(1))
                if not (isinstance(s.i, int) and s.count() < 2):
                    pe.wait_ge(wt_ready, s.count(-1))
                if s.q == 2:
                    head_sums(Step(s.i, s.u0 - 3))
                for b in range(s.q + 1):
                    l = pe.transpose(pa[:, s.par, b * P:(b + 1) * P], probs[s.par][:, 0, b * P:(b + 1) * P],
                                     ident[:, :])
                l.then_inc(w_turned, 1)

            def values(s):
                if not s.exists():
                    return
                pe.wait_ge(wt_ready, s.count(1))
                if s.first and not (isinstance(s.i, int) and s.head() < 2):
                    pe.wait_ge(o_copied, s.head(-1))
                for b in range(s.q + 1):
                    l = pe.matmul(pa[:, 2 + s.h, s.q * P:(s.q + 1) * P], v_cur[s.h][:, b, :],
                                  w_t[s.par][:, b * P:(b + 1) * P], start=b == 0, stop=b == s.q)
                l.then_inc(pv_done, 1)

            def body(i):
                if isinstance(i, int) and i == 0:
                    logits(pe, Step(0, 1))
                for u in range(8):
                    early = u % 4 == 2
                    if early:
                        values(Step(i, u - 1))
                    logits(pe, Step(i, u + 2))
                    turn(Step(i, u))
                    if not early:
                        values(Step(i, u - 1))
            pe.wait_ge(pair_free, at["q"][1] + at["q"][2])
            att_bodies(pe, body)
            values(Step(3, 7))
            pe.wait_ge(wt_ready, AH * NC)
            head_sums(Step(3, 7))
            pe.wait_ge(o_inv_ready, 1)
            for h in range(AH):
                if h >= 2:
                    pe.wait_ge(o_normed, h - 1)
                for c in range(NC):
                    l = pe.matmul(pa[:, 2 + h % 2, c * P:(c + 1) * P],
                                  oinv[:, h, c:c + 1].broadcast_to((P, P)), ident[:, :],
                                  start=True, stop=True)
                l.then_inc(o_spread, 1)

        def exps(act, s):
            if not s.exists():
                return
            act.wait_ge(bias_ready, s.count(1))
            if not (isinstance(s.i, int) and s.count() < 2):
                act.wait_ge(w_turned, s.count(-1))
            for m in range(2):
                act.activation(probs[s.par][:, m, 0:s.n], pw[:, 2 * s.par + m, 0:s.n], ACT.Exp,
                               bias=nb[s.par][:, m:m + 1],
                               accum_out=rs[s.par][:, m:m + 1]).then_inc(exp_ready, 1)

        def att_act(act):
            act.wait_ge(lam_step, 2)
            act.activation(lam_s[:, :], lam_s[:, :], ACT.Exp).then_inc(lam_exp, 1)

            def copy_turned(s):
                act.wait_ge(w_turned, s.count(1))
                if not (isinstance(s.i, int) and s.count() < 2):
                    act.wait_ge(pv_done, s.count(-1))
                act.activation(w_t[s.par][:, 0:s.n], pa[:, s.par, 0:s.n], ACT.Copy).then_inc(wt_ready, 1)

            def copy_o(s):
                if not s.exists():
                    return
                h = s.head()
                if not (isinstance(h, int) and h < 1):
                    act.wait_ge(o_summed, h)
                act.wait_ge(pv_done, s.count(1))
                act.activation(buf_b[:, s.h, :], pa[:, 2 + s.h, :], ACT.Square).then_inc(o_squared, 1)
                act.activation(o_all[:, bass.ds(h, 1), :].squeeze(1) if not isinstance(h, int) else
                               o_all[:, h, :], pa[:, 2 + s.h, :], ACT.Copy).then_inc(o_copied, 1)

            def body(i):
                for u in range(8):
                    exps(act, Step(i, u + 1))
                    copy_turned(Step(i, u))
                    if u in (1, 5):
                        copy_o(Step(i, u - 2))
            att_bodies(act, body)
            copy_o(Step(3, 7))
            act.wait_ge(o_summed, AH)
            act.activation(orms[:, :, :], pa[:, 0, SUMS:SUMS + AH * NC], ACT.Sqrt, bias=eps_col[:, :],
                           scale=1.0 / P).then_inc(o_rms_ready, 1)
            for h in range(AH):
                act.wait_ge(o_normed, h + 1)
                act.activation(o_hi[:, h, :], o_all[:, h, :], ACT.Copy).then_inc(o_hi_ready, 1)

        def row_max(dve, s):
            if not s.exists():
                return
            dve.wait_ge(logits_ready, s.count(1))
            z = pw[:, 2 * s.par:2 * s.par + 2, :]
            dve.memset(z[0:CHUNK, :, s.n - CHUNK:s.n], -1e30).then_inc(masked, 1)
            dve.wait_ge(masked, s.count(1))
            dve.tensor_reduce(nb[s.par][:, :], z[:, :, 0:s.n], AXX, ALU.max, negate=True)\
                .then_inc(bias_ready, 1)

        def att_dve(dve):
            dve.wait_ge(lam_loaded, 16)
            for v in range(2):
                dve.tensor_tensor_reduce(lam_pr[:, v, :], lam_in[:, 2 * v, :], lam_in[:, 2 * v + 1, :],
                                         1.0, 0.0, ALU.mult, ALU.add, lam_s[:, v:v + 1]).then_inc(lam_step, 1)
            dve.wait_ge(lam_exp, 1)
            dve.tensor_tensor(lam[:, :], lam_s[:, 0:1], lam_s[:, 1:2], ALU.subtract).then_inc(lam_step, 1)
            dve.wait_ge(lam_step, 3)
            dve.tensor_scalar(lam[:, :], lam[:, :], LAMBDA_INIT, None, ALU.add).then_inc(lam_step, 1)
            dve.tensor_scalar(g_sub[:, :], gains[:, G["subln"]:G["subln"] + 1], 1.0 - LAMBDA_INIT,
                              None, ALU.mult).then_inc(lam_step, 1)
            dve.wait_ge(lam_step, 5)

            def combine(s):
                dve.wait_ge(exp_ready, s.count(1) * 2)
                dve.reciprocal(ri[s.par][:, :], rs[s.par][:, :]).then_inc(inv_rows, 1)
                dve.wait_ge(inv_rows, s.count(1))
                dve.tensor_tensor(c1[s.par][:, :], ri[s.par][:, 1:2], lam[:, :], ALU.mult)\
                    .then_inc(lam_rows, 1)
                dve.wait_ge(lam_rows, s.count(1))
                p0, p1 = probs[s.par][:, 0, 0:s.n], probs[s.par][:, 1, 0:s.n]
                dve.tensor_scalar(p1, p1, c1[s.par][:, :], None, ALU.mult).then_inc(second_ready, 1)
                dve.wait_ge(second_ready, s.count(1))
                dve.scalar_tensor_tensor(p0, p0, ri[s.par][:, 0:1], p1, ALU.mult, ALU.subtract)\
                    .then_inc(w_ready, 1)

            def body(i):
                for u in range(8):
                    row_max(dve, Step(i, u + 1))
                    combine(Step(i, u))
            att_bodies(dve, body)
            dve.wait_ge(o_rms_ready, 1)
            dve.reciprocal(oinv[:, :, :], orms[:, :, :]).then_inc(o_inv_ready, 1)

            def normed(h):
                dve.wait_ge(o_spread, h + 1)
                dve.scalar_tensor_tensor(o_all[:, h, :], o_all[:, h, :], g_sub[:, :], pa[:, 2 + h % 2, :],
                                         ALU.mult, ALU.mult).then_inc(o_normed, 1)
            normed(0)
            for h in range(AH):
                if h + 1 < AH:
                    normed(h + 1)
                dve.wait_ge(o_hi_ready, h + 1)
                dve.tensor_tensor(o_lo[:, h, :], o_all[:, h, :], o_hi[:, h, :].bitcast(F32),
                                  ALU.subtract).then_inc(o_split, 1)

        def att_sp(sp):
            sp.wait_ge(heads_stored[0], 16 * 6)
            sp.wait_ge(heads_stored[1], 16 * 5)
            sp.dma_start(lam_in[:, :, :], t["attn_lambda"][0].rearrange("a b -> (a b)")
                         .partition_broadcast(P)).then_inc(lam_loaded, 16)

            def head(i, r):
                h = i * 2 + r
                if not (isinstance(i, int) and i == 0):
                    sp.wait_ge(pv_done, i * 8 + (4 * r - 4))
                for dst, src in ((q_cur[r][:, :], q_dram), (k_cur[r][:, :], k_dram),
                                 (v_cur[r][:, :, :].rearrange("p c e -> p (c e)"), v_dram)):
                    sp.dma_start(dst, src[h] if isinstance(h, int) else
                                 src[bass.ds(h, 1)].rearrange("o p x -> (o p) x"))\
                        .then_inc(head_loaded[r], 16)
            head(0, 0)
            head(0, 1)
            for r in range(2):
                sp.wait_ge(heads_stored[r], 16 * 7)
            with sp.Fori(1, 4) as i:
                head(i, 0)
                head(i, 1)

        cum_ready_v = sem("dt_scaled")

        block = ctx.enter_context(nc.Block())
        ffn_w = {"in0": t["ffn1_w_in"][0], "out0": t["ffn1_w_out"][0],
                 "in1": t["ffn2_w_in"][0], "out1": t["ffn2_w_out"][0],
                 "in2": t["ffn1_w_in"][1], "out2": t["ffn1_w_out"][1],
                 "in3": t["ffn2_w_in"][1], "out3": t["ffn2_w_out"][1]}

        @block.sync
        def _(sp):
            load_x(sp, 0)
            load_x(sp, 1)
            for name in phases:
                if name.startswith("in"):
                    ffn_in_sp(sp, name, ffn_w[name])
                elif name.startswith("out"):
                    out_sp(sp, name, ffn_w[name], KF)
                elif name == "ssm":
                    ssm_sp(sp)
                elif name == "sout":
                    out_sp(sp, name, t["ssm_w_out"][0], KI)
                elif name == "kv":
                    pair_sp(sp, name, t["w_kv"])
                elif name == "q":
                    pair_sp(sp, name, t["attn_w_q"][0])
                elif name == "wo":
                    out_sp(sp, name, t["attn_w_o"][0], AH, between=lambda: att_sp(sp))
            out = t["out"][0].rearrange("(t p) d -> p t d", p=P)
            for i in range(S // P):
                sp.wait_ge(left_ready, i + 1)
                sp.wait_ge(right_ready, i + 1)
                sp.dma_start(out[:, i, :], x_out[:, i, :]).then_inc(stored, 16)
            sp.wait_ge(stored, 16 * (S // P))

        @block.gpsimd
        def _(pool):
            pool.memset(ident[:, :], 0.0).then_inc(const_made, 1)
            pool.memset(ones[:, :], 1.0).then_inc(const_made, 1)
            pool.wait_ge(const_made, 2)
            pool.affine_select(out=ident[:, :], in_=ident[:, :], compare_op=ALU.not_equal, fill=1.0,
                               base=0, pattern=[[-1, P]], channel_multiplier=1)\
                .then_inc(const_made, 1)
            pool.affine_select(out=mask[:, :], in_=ones[:, :], compare_op=ALU.is_ge, fill=0.0,
                               base=0, pattern=[[1, P]], channel_multiplier=-1)\
                .then_inc(const_made, 1)
            for p in range(1, X_PAIRS - 1):
                pool.wait_ge(squared, p)
                pool.tensor_tensor(buf_b[:, :, :], buf_b[:, :, :], buf_a[:, :, :], ALU.add)\
                    .then_inc(summed, 1)
            halve(pool, 0)
            for name in phases:
                if name == "ssm":
                    ssm_pool(pool)
                if name.startswith("out") or name in ("sout", "wo"):
                    out_pool(pool, name)

        @block.scalar
        def _(act):
            act.dma_start(first_rows[:, :], t["ffn1_norm"].flatten().rearrange("(r c) -> r c", c=P))\
                .then_inc(first_gains_loaded, 16)
            for p in range(X_PAIRS):
                act.wait_ge(x_turned, p + 1)
                act.activation(x[:, 2 * p:2 * p + 2, :], turned_banks(p), ACT.Copy).then_inc(pair_free, 1)
                if p:
                    hi(act, Units(0, 0, 4), p - 1)
            act.activation(buf_b[:, :, :], x[:, 0:2, :], ACT.Square).then_inc(summed, 1)
            for p in range(1, X_PAIRS):
                sq_act(act, 0, p, p)
            for name in phases:
                if name.startswith("in"):
                    ffn_in_act(act, name)
                elif name == "ssm":
                    ssm_act(act)
                elif name == "kv":
                    pair_act(act, name)
                elif name == "q":
                    pair_act(act, name)
                    att_act(act)
                elif name.startswith("out") or name in ("sout", "wo"):
                    out_act(act, name)
            rms_act(act, state_of[last] + 1)
            act.wait_ge(inv_ready, state_of[last] + 2)
            act.wait_ge(y_turned, X_PAIRS)
            for i in range(S // P):
                act.activation(x_out[:, i, 768:D], out_block(3)[:, i, :], ACT.Identity,
                               bias=zero_col[:, :], scale=inv_tok[:, i:i + 1]).then_inc(right_ready, 1)

        @block.vector
        def _(dve):
            dve.memset(eps_col[:, :], EPS)
            dve.memset(zero_col[:, :], 0.0)
            dve.wait_ge(first_gains_turned, 1)
            dve.tensor_copy(gains[:, 0:16], pa[:, 2, 0:16]).then_inc(first_gains_ready, 1)
            dve.wait_ge(first_gains_ready, 1)
            for p in range(X_PAIRS):
                dve.wait_ge(pair_free, p + 1)
                split_x(dve, 0, p, gain_after("start"))
                if p:
                    lo(dve, Units(0, 0, 4), p - 1)
            for name in phases:
                if name.startswith("in"):
                    ffn_in_dve(dve, name)
                elif name.startswith("out"):
                    out_dve(dve, name, 0.5, gain_after(name))
                elif name == "ssm":
                    ssm_dve(dve)
                elif name == "kv":
                    pair_dve(dve, name)
                elif name == "q":
                    pair_dve(dve, name)
                    att_dve(dve)
                elif name in ("sout", "wo"):
                    out_dve(dve, name, 1.0, gain_after(name))
            dve.wait_ge(squared, (final_state + 1) * X_PAIRS - 1)
            dve.tensor_tensor(buf_a[:, 0, :], buf_a[:, 0, :], buf_a[:, 1, :], ALU.add)\
                .then_inc(last_squares, 1)
            dve.wait_ge(rms_ready, state_of[last] + 2)
            dve.reciprocal(inv_tok[:, :], rms_tok[:, :]).then_inc(inv_ready, 1)
            dve.wait_ge(inv_ready, state_of[last] + 2)
            dve.wait_ge(out_copied, X_PAIRS - 1)
            for i in range(S // P):
                dve.tensor_scalar(x_out[:, i, 0:768], x_out[:, i, 0:768], inv_tok[:, i:i + 1], None,
                                  ALU.mult).then_inc(left_ready, 1)

        @block.tensor
        def _(pe):
            pe.wait_ge(const_made, 3)
            pe.wait_ge(first_gains_loaded, 16)
            pe.transpose(pa[:, 2, 0:16], first_rows[:, :], ident[0:16, 0:16]).then_inc(first_gains_turned, 1)
            for p in range(X_PAIRS):
                turn_x(pe, p)
            for name in phases:
                if name.startswith("in"):
                    ffn_in_pe(pe, name)
                elif name.startswith("out"):
                    out_pe(pe, name, KF, hh, hl, ffn_out_ready(pe, name))
                elif name == "ssm":
                    ssm_pe(pe)
                elif name == "sout":
                    out_pe(pe, name, KI, y_hi, y_lo, lambda u: None)
                elif name == "kv":
                    pair_pe(pe, name)
                elif name == "q":
                    pair_pe(pe, name)
                    att_pe(pe)
                elif name == "wo":
                    out_pe(pe, name, AH, o_hi, o_lo, lambda u: pe.wait_ge(o_split, 4 * u + 4))


_INS = ["x", "ffn1_norm", "ffn1_w_in", "ffn1_w_out", "mixer_norm", "ffn2_norm", "ffn2_w_in",
        "ffn2_w_out", "ssm_w_in", "ssm_conv_w", "ssm_conv_b", "ssm_dt_bias", "ssm_a_log", "ssm_d",
        "ssm_norm", "ssm_w_out", "kv_norm", "w_kv", "attn_w_q", "attn_lambda", "attn_subln",
        "attn_w_o", "final_norm"]


def tables():
    half = 32
    inv = np.float32(10000.0) ** (-np.arange(0, 2 * half, 2, dtype=np.float32) / np.float32(2 * half))
    ang = np.arange(S, dtype=np.float32)[None, :] * inv[:, None].astype(np.float32)
    rows = np.arange(P) % half
    rope = np.stack([np.cos(ang)[rows], np.sin(ang)[rows]]).astype(np.float32)
    swap = np.zeros((P, P), np.float32)
    for m in range(P):
        if m % (2 * half) < half:
            swap[m + half, m] = -1.0
        else:
            swap[m - half, m] = 1.0
    return {"rope_tables": rope, "rope_rotation": swap}


def kernel(**inputs):
    import concourse.bacc as bacc
    from concourse.bass_utils import run_bass_kernel_spmd

    nc = bacc.Bacc("TRN2", target_bir_lowering=False, num_devices=1)
    arrays, t = {}, {}
    for name, a in {**{n: inputs[n] for n in _INS}, **tables()}.items():
        a = np.ascontiguousarray(a)
        arrays[f"in_{name}"] = a
        t[name] = nc.dram_tensor(f"in_{name}", a.shape, mybir.dt.from_np(a.dtype),
                                 kind="ExternalInput").ap()
    t["out"] = nc.dram_tensor("out_y", (1, S, D), F32, kind="ExternalOutput").ap()
    build_trunk(nc, t)
    r = run_bass_kernel_spmd(nc, [arrays], core_ids=[0])
    return r.results[0]["out_y"]
```
